# Optimizing a Trainium2 kernel written in Bass

```python
import jax, jax.numpy as jnp
from jax import lax
import numpy as np

D_MODEL = 1024
BATCH = 1
SEQ = 256
DEPTH = 2

GRID_W = 64
CTX_LEN = 256
EPS = 1e-6
ROPE_THETA = 10000.0
Q_BLOCK = 128
N_MOD = 6

CHUNK = 128
A_GROUPS = 4
A_WIDTH = 512
A_HEAD = A_WIDTH // A_GROUPS
B_WIDTH = 512
POOL_WINDOWS = (2, 4, 8, 16)
B_GROUP = B_WIDTH // len(POOL_WINDOWS)
AB_IN = 2 * A_WIDTH + B_WIDTH
AB_OUT = A_WIDTH + B_WIDTH

HEAD_DIM = 64
C_HEADS = 8
C_KV_HEADS = 2
C_Q = C_HEADS * HEAD_DIM
C_KV = C_KV_HEADS * HEAD_DIM
D_HEADS = 8
D_NOPE = 64
D_ROPE = 32
D_V = 64
Q_RANK = 384
KV_RANK = 256
OFF_KC = C_Q
OFF_VC = OFF_KC + C_KV
OFF_CQ = OFF_VC + C_KV
OFF_CKV = OFF_CQ + Q_RANK
OFF_KR = OFF_CKV + KV_RANK
CD_IN = OFF_KR + D_ROPE
CD_OUT = C_HEADS * HEAD_DIM + D_HEADS * D_V

D_FF = 2816
N_EXPERTS = 8
TOP_K = 2
D_FF_EXPERT = 2816

kernel_name = "hybrid_diffusion_prefix_trunk"

def rmsnorm(x, gain=None):
    xf = x.astype(jnp.float32)
    y = xf * lax.rsqrt(jnp.mean(xf * xf, axis=-1, keepdims=True) + EPS)
    if gain is not None:
        y = y * gain.astype(jnp.float32)
    return y.astype(x.dtype)

def modulate(x, shift, scale):
    return rmsnorm(x) * (1 + scale) + shift

def adaln(cvec, w, b):
    m = jax.nn.silu(cvec) @ w + b
    return tuple(jnp.split(m[:, None, :], N_MOD, axis=-1))

def axial_rope(length, rot_dim):
    rows = length // GRID_W
    row = jnp.repeat(jnp.arange(rows), GRID_W).astype(jnp.float32)
    col = jnp.tile(jnp.arange(GRID_W), rows).astype(jnp.float32)
    axis_dim = rot_dim // 2
    inv = ROPE_THETA ** (-jnp.arange(0, axis_dim, 2, dtype=jnp.float32) / axis_dim)
    ang = jnp.concatenate([row[:, None] * inv, col[:, None] * inv], axis=-1)
    return jnp.cos(ang), jnp.sin(ang)

def apply_rope(x, cos, sin):
    half = x.shape[-1] // 2
    shape = (1, x.shape[1]) + (1,) * (x.ndim - 3) + (half,)
    c = cos.reshape(shape).astype(x.dtype)
    s = sin.reshape(shape).astype(x.dtype)
    x1, x2 = x[..., :half], x[..., half:]
    return jnp.concatenate([x1 * c - x2 * s, x1 * s + x2 * c], axis=-1)

def block_attention(q, k, v, scale):
    b, lq, hkv, g, dk = q.shape
    nb = lq // Q_BLOCK
    qb = q.reshape(b, nb, Q_BLOCK, hkv, g, dk).transpose(1, 0, 2, 3, 4, 5)

    def one_block(qblk):
        s = jnp.einsum('bqhgd,bkhd->bhgqk', qblk, k, preferred_element_type=jnp.float32) * scale
        p = jax.nn.softmax(s, axis=-1).astype(v.dtype)
        return jnp.einsum('bhgqk,bkhd->bqhgd', p, v)

    o = lax.map(one_block, qb)
    return o.transpose(1, 0, 2, 3, 4, 5).reshape(b, lq, -1)

def chunk_gmlp(a, v_gain, w_s, b_s):
    u, v = a[..., :A_WIDTH], a[..., A_WIDTH:]
    v = rmsnorm(v, v_gain)
    b, l, _ = v.shape
    vc = v.reshape(b, l // CHUNK, CHUNK, A_GROUPS, A_HEAD)
    s = jnp.einsum('gpq,bcqgd->bcpgd', w_s, vc) + b_s.T[:, :, None]
    return u * s.reshape(b, l, A_WIDTH)

def multiscale_pool(z, w_pool, scale):
    b, l, _ = z.shape
    zf = z.astype(jnp.float32)
    cs = jnp.concatenate([jnp.zeros((b, 1, B_WIDTH), jnp.float32), jnp.cumsum(zf, axis=1)], axis=1)
    pos = jnp.arange(l)
    outs = []
    for g, w in enumerate(POOL_WINDOWS):
        lo = jnp.clip(pos - w // 2, 0, l)
        hi = jnp.clip(pos - w // 2 + w, 0, l)
        sl = slice(g * B_GROUP, (g + 1) * B_GROUP)
        csg = cs[..., sl]
        mean = (jnp.take(csg, hi, axis=1) - jnp.take(csg, lo, axis=1)) / (hi - lo).astype(jnp.float32)[None, :, None]
        outs.append((mean - zf[..., sl]).astype(z.dtype))
    pooled = jnp.stack(outs, axis=2)
    y = jnp.einsum('blgi,gio->blgo', pooled, w_pool).reshape(b, l, B_WIDTH)
    return y * scale

def ab_mixer(h, w_in, v_gain, w_s, b_s, w_pool, p_scale, w_out):
    z = h @ w_in
    ya = chunk_gmlp(jax.nn.gelu(z[..., :2 * A_WIDTH], approximate=False), v_gain, w_s, b_s)
    yb = multiscale_pool(z[..., 2 * A_WIDTH:], w_pool, p_scale)
    return jnp.concatenate([ya, yb], axis=-1) @ w_out

def cd_queries(z, q_gain, cq_gain, w_uq, rope_c, rope_d):
    b, l, _ = z.shape
    qc = rmsnorm(z[..., :OFF_KC].reshape(b, l, C_HEADS, HEAD_DIM), q_gain)
    qd = (rmsnorm(z[..., OFF_CQ:OFF_CKV], cq_gain) @ w_uq).reshape(b, l, D_HEADS, D_NOPE + D_ROPE)
    q_nope, q_rope = qd[..., :D_NOPE], qd[..., D_NOPE:]
    if rope_c is not None:
        qc = apply_rope(qc, *rope_c)
        q_rope = apply_rope(q_rope, *rope_d)
    qc = qc.reshape(b, l, C_KV_HEADS, C_HEADS // C_KV_HEADS, HEAD_DIM)
    qd = jnp.concatenate([q_nope, q_rope], axis=-1)[:, :, :, None, :]
    return qc, qd

def cd_keys(z, k_gain, ckv_gain, w_ukv, rope_c, rope_d):
    b, l, _ = z.shape
    kc = rmsnorm(z[..., OFF_KC:OFF_VC].reshape(b, l, C_KV_HEADS, HEAD_DIM), k_gain)
    vc = z[..., OFF_VC:OFF_CQ].reshape(b, l, C_KV_HEADS, HEAD_DIM)
    kv = (rmsnorm(z[..., OFF_CKV:OFF_KR], ckv_gain) @ w_ukv).reshape(b, l, D_HEADS, D_NOPE + D_V)
    kr = z[..., OFF_KR:][:, :, None, :]
    if rope_c is not None:
        kc = apply_rope(kc, *rope_c)
        kr = apply_rope(kr, *rope_d)
    kd = jnp.concatenate([kv[..., :D_NOPE], jnp.broadcast_to(kr, (b, l, D_HEADS, D_ROPE))], axis=-1)
    vd = kv[..., D_NOPE:]
    return kc, vc, kd, vd

def cd_attend(qc, qd, kc, vc, kd, vd, w_out):
    oc = block_attention(qc, kc, vc, HEAD_DIM ** -0.5)
    od = block_attention(qd, kd, vd, (D_NOPE + D_ROPE) ** -0.5)
    return jnp.concatenate([oc, od], axis=-1) @ w_out

def swiglu(h, w_gate, w_up, w_down):
    return (jax.nn.silu(h @ w_gate) * (h @ w_up)) @ w_down

def moe_swiglu(h, router, w_gate, w_up, w_down):
    b, l, d = h.shape
    hf = h.reshape(-1, d)
    logits = (hf @ router).astype(jnp.float32)
    top_v, top_i = lax.top_k(logits, TOP_K)
    top_w = jax.nn.softmax(top_v, axis=-1)
    gates = jnp.sum(jax.nn.one_hot(top_i, N_EXPERTS, dtype=jnp.float32) * top_w[..., None], axis=1).astype(h.dtype)
    y = jnp.zeros_like(hf)
    for e in range(N_EXPERTS):
        y = y + gates[:, e:e + 1] * swiglu(hf, w_gate[e], w_up[e], w_down[e])
    return y.reshape(b, l, d)

def setup_inputs(seed: int = 0) -> dict:
    key = jax.random.key(seed)
    ks = iter(jax.random.split(key, 32))
    n_even = (DEPTH + 1) // 2
    n_odd = DEPTH // 2
    D = D_MODEL

    def nrm(shape, scale):
        return scale * jax.random.normal(next(ks), shape, jnp.float32)

    def gain(shape):
        return 1.0 + 0.1 * jax.random.normal(next(ks), shape, jnp.float32)

    return {
        "x": nrm((BATCH, SEQ, D), 1.0),
        "c": nrm((BATCH, D), 1.0),
        "ctx": nrm((BATCH, CTX_LEN, D), 1.0),
        "c_ctx": nrm((D,), 1.0),
        "ada_w": nrm((DEPTH, D, N_MOD * D), D ** -0.5),
        "ada_b": nrm((DEPTH, N_MOD * D), 0.02),
        "ab_w_in": nrm((n_even, D, AB_IN), D ** -0.5),
        "a_v_gain": gain((n_even, A_WIDTH)),
        "a_w_s": nrm((n_even, A_GROUPS, CHUNK, CHUNK), CHUNK ** -0.5),
        "a_b_s": gain((n_even, A_GROUPS, CHUNK)),
        "b_w_pool": nrm((n_even, len(POOL_WINDOWS), B_GROUP, B_GROUP), B_GROUP ** -0.5),
        "b_scale": gain((n_even, B_WIDTH)),
        "ab_w_out": nrm((n_even, AB_OUT, D), AB_OUT ** -0.5),
        "ffn_w_gate": nrm((n_even, D, D_FF), D ** -0.5),
        "ffn_w_up": nrm((n_even, D, D_FF), D ** -0.5),
        "ffn_w_down": nrm((n_even, D_FF, D), D_FF ** -0.5),
        "cd_w_in": nrm((n_odd, D, CD_IN), D ** -0.5),
        "c_q_gain": gain((n_odd, HEAD_DIM)),
        "c_k_gain": gain((n_odd, HEAD_DIM)),
        "d_cq_gain": gain((n_odd, Q_RANK)),
        "d_ckv_gain": gain((n_odd, KV_RANK)),
        "d_w_uq": nrm((n_odd, Q_RANK, D_HEADS * (D_NOPE + D_ROPE)), Q_RANK ** -0.5),
        "d_w_ukv": nrm((n_odd, KV_RANK, D_HEADS * (D_NOPE + D_V)), KV_RANK ** -0.5),
        "cd_w_out": nrm((n_odd, CD_OUT, D), CD_OUT ** -0.5),
        "moe_router": nrm((n_odd, D, N_EXPERTS), D ** -0.5),
        "moe_w_gate": nrm((n_odd, N_EXPERTS, D, D_FF_EXPERT), D ** -0.5),
        "moe_w_up": nrm((n_odd, N_EXPERTS, D, D_FF_EXPERT), D ** -0.5),
        "moe_w_down": nrm((n_odd, N_EXPERTS, D_FF_EXPERT, D), D_FF_EXPERT ** -0.5),
        "final_gain": gain((D,)),
    }

def reference(x, c, ctx, c_ctx, ada_w, ada_b, ab_w_in, a_v_gain, a_w_s, a_b_s, b_w_pool, b_scale, ab_w_out,
              ffn_w_gate, ffn_w_up, ffn_w_down, cd_w_in, c_q_gain, c_k_gain, d_cq_gain, d_ckv_gain, d_w_uq,
              d_w_ukv, cd_w_out, moe_router, moe_w_gate, moe_w_up, moe_w_down, final_gain):
    seq = x.shape[1]
    rope_c = axial_rope(seq, HEAD_DIM)
    rope_d = axial_rope(seq, D_ROPE)
    t = ctx
    ctx_len = ctx.shape[1]

    def cat(a, b):
        return jnp.concatenate([a, b], axis=1)

    for layer in range(DEPTH):
        last = layer == DEPTH - 1
        odd = layer % 2 == 1
        i = layer // 2
        sh1, sc1, g1, sh2, sc2, g2 = adaln(c, ada_w[layer], ada_b[layer])
        if odd or not last:
            tsh1, tsc1, tg1, tsh2, tsc2, tg2 = adaln(c_ctx[None, :], ada_w[layer], ada_b[layer])
            ht = modulate(t, tsh1, tsc1)
        hx = modulate(x, sh1, sc1)

        if not odd:
            ab = (ab_w_in[i], a_v_gain[i], a_w_s[i], a_b_s[i], b_w_pool[i], b_scale[i], ab_w_out[i])
            mx = ab_mixer(hx, *ab)
            if not last:
                mt = ab_mixer(ht, *ab)
        else:
            zx = hx @ cd_w_in[i]
            zt = ht @ cd_w_in[i]
            qcx, qdx = cd_queries(zx, c_q_gain[i], d_cq_gain[i], d_w_uq[i], rope_c, rope_d)
            kcx, vcx, kdx, vdx = cd_keys(zx, c_k_gain[i], d_ckv_gain[i], d_w_ukv[i], rope_c, rope_d)
            kct, vct, kdt, vdt = cd_keys(zt, c_k_gain[i], d_ckv_gain[i], d_w_ukv[i], None, None)
            mx = cd_attend(qcx, qdx, cat(kct, kcx), cat(vct, vcx), cat(kdt, kdx), cat(vdt, vdx), cd_w_out[i])
            if not last:
                qct, qdt = cd_queries(zt, c_q_gain[i], d_cq_gain[i], d_w_uq[i], None, None)
                mt = cd_attend(qct, qdt, kct, vct, kdt, vdt, cd_w_out[i])
        x = x + g1 * mx
        if not last:
            t = t + tg1 * mt

        hx2 = modulate(x, sh2, sc2)
        h2 = hx2 if last else cat(modulate(t, tsh2, tsc2), hx2)
        if odd:
            f = moe_swiglu(h2, moe_router[i], moe_w_gate[i], moe_w_up[i], moe_w_down[i])
        else:
            f = swiglu(h2, ffn_w_gate[i], ffn_w_up[i], ffn_w_down[i])
        if last:
            x = x + g2 * f
        else:
            t = t + tg2 * f[:, :ctx_len]
            x = x + g2 * f[:, ctx_len:]

    return rmsnorm(x, final_gain)


_drawn_inputs = setup_inputs


def setup_inputs(seed=0):
    import zlib

    import numpy as np

    out = dict(_drawn_inputs(seed))
    spreads = {}
    factors = {'c_q_gain': 8.0, 'c_k_gain': 7.016, 'd_cq_gain': 3.794}
    for name, (base, spread) in spreads.items():
        noise = np.random.default_rng([zlib.crc32(name.encode()), seed]).standard_normal(out[name].shape)
        drawn = base * np.exp(spread * noise) if base else spread * noise
        out[name] = __import__('jax').numpy.asarray(drawn.astype(out[name].dtype))
    for name, factor in factors.items():
        out[name] = (out[name] * factor).astype(out[name].dtype)
    return out
```

```python
from contextlib import ExitStack

import numpy as np

import concourse.bass as bass
from concourse import mybir

F32 = mybir.dt.float32
F32R = mybir.dt.float32r
I32 = mybir.dt.int32
U32 = mybir.dt.uint32
ALU = mybir.AluOpType
ACT = mybir.ActivationFunctionType
AX = mybir.AxisListType.X

P = 128
D = 1024
KD = D // P
SEQ = 256
NT = 4
EPS = 1e-6
GRID_W = 64
ROPE_THETA = 10000.0
AW = 512
POOL_WINDOWS = (2, 4, 8, 16)
FF = 2816
NE = 8
SLOTS = 128
ROUNDS = SEQ // SLOTS
CAP = SLOTS
OVER = 2 * SEQ // (SLOTS + 1)
GATE_BLOCKS = (4, 5, 10, 11)
KIND = {0: 0, 1: 1, 3: 2, 4: 3}
LOOP_KEYS = (("uA", "dA", "gA"), ("uB", "dB", "gB"))
OUT_KEYS = (("u9", "d8", "g10"), ("u10", "d9", "d10"))
CD_TILES = [range(4) if j in (2, 4, 5) else range(2, 4) for j in range(6)]
ZT0 = {2: 0, 4: 256, 5: 512}
CQ0, CKV0, KR0, CDIN = 768, 1152, 1408, 1440
RAW, SPL = 6, 3
SLAB = 2048
FFI = FF // 256


def slab_order():
    ffn = [("ffn_in", 1, ["g0", "u0", "g1"]),
           ("ffn_loop", 4, ["uA", "dA", "gA", "uB", "dB", "gB"]),
           ("ffn_out", 1, ["u9", "d8", "g10", "u10", "d9", "d10"])]
    expert = [(w, s) for w in range(2) for s in range(33)]
    return ([("ada0", 1, [(cb, h) for cb in range(12) for h in range(2)]),
             ("ab_in", 1, list(range(6))), ("ab_out", 1, [(h, q) for h in range(2) for q in range(2)])] + ffn +
            [("ada1", 1, [(cb, h) for cb in range(12) for h in range(2)]),
             ("cd_in", 1, list(range(6))), ("uq", 1, [0, 1]), ("ukv", 1, [0]),
             ("cd_out", 1, [(h, q) for h in range(2) for q in range(2)])] +
            [("moe", NE // 2, expert), ("over", OVER, [(0, s) for s in range(33)])])


def bank_order():
    out = []

    def ada(layer):
        rows = [(("m", cb), cb % 2, (cb, 1)) for cb in range(12)]
        cols = []
        for cb in range(12):
            if cb // 2 in (2, 5):
                cols += [(("bc", cb, 0), 2)] + ([(("bc", cb, 1), 3)] if layer == 0 else [])
            else:
                cols.append((("col", cb), 4 + cb % 2))
        return (f"ada{layer}", 1, rows + cols)

    out.append(("start", 1, [("cT", 0), ("wsT", 1)]))
    out.append(ada(0))
    out.append(("norm0", 1, [(k, k) for k in range(8)]))
    out.append(("ab_in", 1, [((j, t), (4 * j + t) % 8) + ((j,) if t == 3 else ()) for j in range(6) for t in range(NT)]))
    out.append(("ab_s", 1, [(t, t) for t in range(NT)]))
    out.append(("ab_pool", 1, [(g, g) for g in range(4)]))
    out.append(("ab_yb", 1, [(g, 4 + g) for g in range(4)]))
    out.append(("ab_ya", 1, [(g, 4 + g) for g in range(4)]))
    out.append(("ab_out", 1, [((h, t), 4 * h + t) + (((h, 1),) if t == 3 else ()) for h in range(2) for t in range(NT)]))
    out.append(("norm1", 1, [(k, k) for k in range(8)]))

    out.append(("ffn", FFI, [((kind, b), n + b) + ((kind,) if b else ()) for kind, n in (("g", 0), ("u", 2)) for b in range(2)] +
                [(("d", o), 4 + o % 4) + (("d",) if o == 7 else ()) for o in range(8)]))
    out.append(ada(1))
    out.append(("norm2", 1, [(k, k) for k in range(8)]))
    uses = [(j, t) for j in range(6) for t in range(NT) if t >= 2 or j in (2, 4, 5)]
    out.append(("cd_in", 1, [(u, n % 8) + ((u[0],) if u[1] == 3 else ()) for n, u in enumerate(uses)]))
    out.append(("cq", 1, [(b, b) for b in range(3)]))
    out.append(("ckv", 1, [(b, 4 + b) for b in range(2)]))
    out.append(("uq", 1, [((h, a), 2 * h + a) + ((h,) if a else ()) for h in range(2) for a in range(2)]))
    out.append(("ukv", 1, [((t, h), (4 + 2 * t + h) % 8) + ((0,) if (t, h) == (3, 1) else ()) for t in range(NT) for h in range(2)]))
    out.append(("heads", 1, [("kc", 0), (("qc", 0), 1), (("qc", 1), 2), ("kr", 3)] +
                [(("kd", h), 4 + h % 4) for h in range(8)] + [(("qd", h), h % 4) for h in range(4)]))
    att = []
    for i in range(34):
        if i < 32:
            att.append((("s", i), i % 3))
        if 2 <= i:
            att.append((("o", i - 2), 5 + i % 2))
        if 1 <= i < 33:
            att.append((("t", i - 1), 3 + (i - 1) % 2))
    out.append(("att", 1, att))
    out.append(("oT", 1, [(b, b) for b in range(4)]))
    out.append(("cd_out", 1, [((h, a), 4 + 2 * h + a) + (((h, 1),) if a else ()) for h in range(2) for a in range(2)]))
    out.append(("norm3", 1, [(k, k) for k in range(8)]))
    out.append(("route", 1, [("logits", 0), ("cum", 1), (("back", 0), 2), (("back", 1), 3), (("back", 2), 4),
                             (("back", 3), 5)]))

    def gather(w):
        return [(("xh", w, 0), 5), (("xh", w, 1), 4), (("xl", w, 0), 5), (("xl", w, 1), 4), (("pt", w), 5)]

    def scatter(w):
        return [(("y", w, o), 5 - o % 2) for o in range(4)]

    def expert(w, middle, between):
        body = []
        for c in range(6):
            body += [(("g", w, c), c % 2, (w, 4 * c + 1 if c < 5 else 20)), (("u", w, c), 2 + c % 2, (w, 4 * c + 3 if c < 5 else 21))]
            if c == 0:
                body += middle
            if c >= 1:
                body.append((("t", w, c - 1), 4 + (c - 1) % 2))
        return body + between + [(("t", w, 5), 4), (("d", w, 0), 6), (("d", w, 1), 7, (w, 32))]
    out.append(("first", 1, gather(1)))
    out.append(("moe", NE // 2, expert(0, [], gather(0)) + expert(1, scatter(0), gather(1)) + scatter(1)))
    out.append(("over", OVER, gather(1) + expert(0, [], []) + scatter(0)))
    return out


def shape_tables():
    f = np.float32
    t = {}
    sel = np.zeros((5, 2, P), f)
    for who in range(2):
        sel[[who, who + 2, 4], who, :] = 1
    t["k_sel"] = sel
    t["k_ident"] = np.eye(P, dtype=f)
    t["k_ones"] = np.ones((P, P), f)
    t["k_tri"] = np.triu(np.ones((P, P), f))
    t["k_slot"] = np.tile(np.arange(ROUNDS * SLOTS, dtype=f), (P, 1))
    t["k_expert"] = np.tile(np.arange(NE, dtype=f), (P, 1))
    band = np.zeros((SEQ, 4, SEQ), f)
    pos = np.arange(SEQ)
    for g, w in enumerate(POOL_WINDOWS):
        lo = np.clip(pos - w // 2, 0, SEQ)
        hi = np.clip(pos - w // 2 + w, 0, SEQ)
        inside = (pos[:, None] >= lo[None]) & (pos[:, None] < hi[None])
        band[:, g] = np.where(inside, f(1) / (hi - lo).astype(f), f(0)) - np.eye(SEQ, dtype=f)
    t["k_band"] = np.stack([band[a * P:(a + 1) * P, :, a * 112:a * 112 + 144] for a in range(2)], 2).copy()
    rows = np.repeat(np.arange(SEQ // GRID_W), GRID_W).astype(f)
    cols = np.tile(np.arange(GRID_W), SEQ // GRID_W).astype(f)
    for name, dim in (("k_ropec", 64), ("k_roped", 32)):
        axis = dim // 2
        inv = (f(ROPE_THETA) ** (-np.arange(0, axis, 2, dtype=f) / f(axis))).astype(f)
        ang = np.concatenate([rows[:, None] * inv, cols[:, None] * inv], -1)
        c, s = np.cos(ang), np.sin(ang)
        both = np.stack([np.concatenate([c, c], -1), np.concatenate([-s, s], -1)], 1)
        t[name] = both.reshape(2, P, 2, dim).transpose(1, 0, 2, 3).astype(f).copy()
    return t


class Count:

    def __init__(self, eng, sem):
        self.eng, self.sem, self.n, self.it, self.per, self.at = eng, sem, 0, None, 0, 0

    def mark(self, ins):
        ins.then_inc(self.sem, 1)
        self.n += 1

    def wait(self):
        self.eng.wait_ge(self.sem, self.n if self.it is None else self.it * self.per + self.n)

    def enter(self, it, per):
        self.it, self.per, self.at = it, per, self.n

    def leave(self, times):
        assert self.n - self.at == self.per, (self.n - self.at, self.per)
        self.n, self.it = self.at + times * self.per, None


def build(nc, a, out):
    slabs, n, landed = {}, 0, [0] * RAW
    for stage, times, keys in slab_order():
        depth = RAW if times == 1 or len(keys) % RAW == 0 else SPL
        assert times == 1 or len(keys) % depth == 0
        slots = [(n + i) % depth for i in range(len(keys))]
        for i, key in enumerate(keys):
            slabs[stage, key] = (n + i, len(keys), slots[i], landed[slots[i]] + slots[:i].count(slots[i]),
                                 slots.count(slots[i]), depth)
        landed = [landed[b] + times * slots.count(b) for b in range(RAW)]
        n += times * len(keys)
    banks, at, signals = {}, [0] * 8, [0] * 8
    for stage, times, uses in bank_order():
        per = [sum(u[1] == b for u in uses) for b in range(8)]
        per_signal = [sum(u[1] == b and len(u) == 2 for u in uses) for b in range(8)]
        use, signal = list(at), list(signals)
        for key, b, *closing in uses:
            assert (stage, key) not in banks
            banks[stage, key] = (b, use[b], per[b], signal[b], per_signal[b], closing[0] if closing else None)
            use[b] += 1
            signal[b] += not closing
        at = [at[b] + times * per[b] for b in range(8)]
        signals = [signals[b] + times * per_signal[b] for b in range(8)]

    with ExitStack() as ctx:
        def sem(name):
            return ctx.enter_context(nc.semaphore(name))

        def sb(name, shape, dt=F32, into=None):
            return (into or ctx).enter_context(nc.sbuf_tensor(name, shape, dt))

        raw = [sb(f"raw{i}", [P, SLAB]) for i in range(RAW)]
        hi = [sb(f"hi{i}", [P, SLAB], F32R) for i in range(SPL)]
        lo = [sb(f"lo{i}", [P, SLAB], F32R) for i in range(SPL)]
        X = sb("X", [P, NT, D])
        ident = sb("ident", [P, P])
        sel = sb("sel", [5, 2, P])
        crows = sb("crows", [29, P])
        C4 = sb("C4", [P, KD, 4], F32R)
        cs = sb("cs", [P, 16])
        mrow = sb("mrow", [P, 2, 512])
        modcol = [sb(f"modcol{i}", [P, 4, KD, 2]) for i in range(2)]
        ropec = sb("ropec", [P, 2, 2, 64])
        roped = sb("roped", [P, 2, 2, 32])
        q_gain = sb("q_gain", [P, 64])
        k_gain = sb("k_gain", [P, 64])
        pcols = sb("pcols", [P, 13])
        bs_col, bscale_col, cq_gain, ckv_gain = pcols[:, 0:4], pcols[:, 4:8], pcols[:, 8:11], pcols[:, 11:13]
        ssq = sb("ssq", [P, NT, 12])
        rstd = sb("rstd", [P, NT, 12])
        root = sb("root", [P, NT, 12])
        rowmax = sb("rowmax", [P, 2, 32])
        rowsum = sb("rowsum", [P, 2, 32])
        ps = [ctx.enter_context(nc.psum_tensor(f"bank{i}", [P, 512], F32)) for i in range(8)]

        zone = ExitStack()
        gates = [sb(f"gate_rows{w}", [P, 2, D], into=zone) for w in range(2)]
        Hhi = sb("Hhi", [P, KD, 512], F32R, zone)
        Hlo = sb("Hlo", [P, KD, 512], F32R, zone)
        free0 = ExitStack()
        u = sb("u", [P, NT, AW], into=free0)
        v = sb("v", [P, NT, AW], into=free0)
        zp = sb("zp", [P, NT, AW], into=free0)
        vgain = sb("vgain", [P, AW], into=free0)
        band = sb("band", [P, 4, 2, 144], into=free0)
        wsT = sb("wsT", [P, 4, P], into=free0)
        wpool = sb("wpool", [P, 4, P], into=free0)
        vsq = mrow[:, 0, :]
        htmpA = zp[:, 0:2, :]
        ws = zp[:, 3, :].rearrange("p (g q) -> p g q", g=4)
        pooledT = v[:, 0:2, :]
        ybtmp = v[:, 2:4, :]
        otmpA = u[:, 0:2, :]
        free0.close()
        free1 = ExitStack()
        acth = sb("acth", [P, 2, 2, 512], F32R, free1)
        actl = sb("actl", [P, 2, 2, 512], F32R, free1)
        yacc = sb("yacc", [P, NT, D], into=free1)
        sg = mrow
        am = sb("am", [P, 2, 512], into=free1)
        free1.close()
        zone.close()
        zone1 = ExitStack()
        gates1 = sb("gates1", [P, 2, D], into=zone1)
        H1hi = sb("H1hi", [P, KD, 512], F32R, zone1)
        H1lo = sb("H1lo", [P, KD, 512], F32R, zone1)
        Zx = sb("Zx", [P, 2, CDIN], into=zone1)
        Zt = sb("Zt", [P, 2, 672], into=zone1)
        qd = sb("qd", [P, 2, 768], into=zone1)
        kv = sb("kv", [P, NT, D], into=zone1)
        pexp = sb("pexp", [P, 2, 512], into=zone1)
        pT = mrow
        zone1.close()
        zone2 = ExitStack()
        sb("gates1_again", [P, 2, D], into=zone2)
        kdT = sb("kdT", [P, 8, 512], into=zone2)
        qdT = sb("qdT", [P, 8, 256], into=zone2)
        kcT = sb("kcT", [P, 512], into=zone2)
        qcT = sb("qcT", [P, 4, 256], into=zone2)
        zone2.close()
        zone3 = ExitStack()
        sb("gates1_third", [P, 2, D], into=zone3)
        oTh = sb("oTh", [P, KD, 256], F32R, zone3)
        oTl = sb("oTl", [P, KD, 256], F32R, zone3)
        zone3.close()
        zone4 = ExitStack()
        sb("gates1_last", [P, 2, D], into=zone4)
        h2h = sb("h2h", [P, 2, D], F32R, zone4)
        h2l = sb("h2l", [P, 2, D], F32R, zone4)
        xgh = sb("xgh", [P, KD, P], F32R, zone4)
        xgl = sb("xgl", [P, KD, P], F32R, zone4)
        yeh = sb("yeh", [P, 2, 512], F32R, zone4)
        yel = sb("yel", [P, 2, 512], F32R, zone4)
        Pm = sb("Pm", [P, 2, 2, P], F32R, zone4)
        PT = sb("PT", [P, 2, 2, P], F32R, zone4)
        sge = sb("sge", [P, 2, 512], into=zone4)
        ame = sb("ame", [P, 2, 512], into=zone4)
        logits = sb("logits", [P, 2, NE], into=zone4)
        top = sb("top", [P, 2, 8], into=zone4)
        topi = sb("topi", [P, 2, 8], U32, zone4)
        topf = sb("topf", [P, 2, 8], into=zone4)
        wts = sb("wts", [P, 2, 4], into=zone4)
        pick = sb("pick", [P, 2, 2, NE], into=zone4)
        chosen = sb("chosen", [P, 2, NE], into=zone4)
        posn = sb("posn", [P, 2, NE + 1], into=zone4)
        gate_e = sb("gate_e", [P, 2, NE], into=zone4)
        over = sb("over", [P, 3, NE], into=zone4)
        over_i = sb("over_i", [P, 2, NE], I32, zone4)
        fgain = sb("fgain", [P, D], into=zone4)
        ones = sb("ones", [P, P], into=zone4)
        tri = sb("tri", [P, P], into=zone4)
        slot_row = sb("slot_row", [P, ROUNDS * SLOTS], into=zone4)
        expert_row = sb("expert_row", [P, NE], into=zone4)
        router = sb("router", [P, KD, NE], into=zone4)
        zone5 = ExitStack()
        h2T = sb("h2T", [P, KD, 256], into=zone5)
        xnM = sb("xnM", [P, 2, D], into=zone5)
        zone5.close()
        aTh = sb("aTh", [P, 22, P], F32R, zone4)
        aTl = sb("aTl", [P, 22, P], F32R, zone4)
        zone4.close()
        yM = X[:, 0:2, :]

        raw_in = [sem(f"raw_in{i}") for i in range(RAW)]
        hi_ready, slab_used = sem("hi_ready"), sem("slab_used")
        lo_dve = [sem(f"lo_dve{i}") for i in range(SPL)]
        lo_pool = [sem(f"lo_pool{i}") for i in range(SPL)]
        bank_full = [sem(f"bank_full{i}") for i in range(8)]
        bank_emptied = [sem(f"bank_emptied{i}") for i in range(8)]
        c_in, sel_in, x_in, ident_in, ab_consts = sem("c_in"), sem("sel_in"), sem("x_in"), sem("ident_in"), sem("ab_consts")
        ssq_clear, cqn_ready, cn_ready, kr_ready, logit_diff = (sem(n_) for n_ in (
            "ssq_clear", "cqn_ready", "cn_ready", "kr_ready", "logit_diff"))
        experts_in = sem("experts_consts_in")
        l1_in, fgain_in, bias_in = sem("layer1_consts_in"), sem("fgain_in"), [sem(f"bias_in{i}") for i in range(2)]
        silu_c, c_hi, c_lo = sem("silu_c"), sem("c_hi"), sem("c_lo")
        dve_chain, act_chain = sem("dve_chain"), sem("act_chain")
        sumsq = [sem(f"sumsq{i}") for i in range(7)]
        meansq = [sem(f"meansq{i}") for i in range(7)]
        rooted = [sem(f"rooted{i}") for i in range(7)]
        xn_ready = [sem(f"xn_ready{i}") for i in range(4)]
        h_tmp = [sem(f"h_tmp{i}") for i in range(4)]
        h_ready = [sem(f"h_ready{i}") for i in range(4)]
        x_ready = [sem(f"x_ready{i}") for i in range(4)]
        v_ready, ya_hi, y_ready = sem("v_ready"), sem("ya_hi"), sem("y_ready")
        ff_ready, qk_ready, kvn_ready = sem("ff_ready"), sem("qk_ready"), sem("kvn_ready")
        cqt_tmp, up_ready, rope_ready = sem("cqt_tmp"), sem("up_ready"), sem("rope_ready")
        kr_copied = sem("kr_copied")
        negmax, exped, o_ready, oT_hi = sem("negmax"), sem("exped"), sem("o_ready"), sem("oT_hi")
        h2_hi, h2_ready, logit_in, routed = sem("h2_hi"), sem("h2_ready"), sem("logit_in"), sem("routed")
        chosen_ready, gexp = sem("chosen_ready"), sem("gate_exp")
        p_ready = [sem(f"p_ready{r}") for r in range(ROUNDS)]
        hi_out = [sem(f"hi_out{r}") for r in range(ROUNDS)]
        summed, y_done, fin_ready, stored = sem("summed"), sem("y_done"), sem("fin_ready"), sem("stored")

        def view(t, shape):
            k, f = shape
            return t[:, 0:k * f].rearrange("p (k f) -> p k f", k=k)

        def load(sp, stage, key, src, it=0):
            n0, per, slot, _, _, depth = slabs[stage, key]
            if n0 >= depth:
                before = (n0 - depth) // SPL + 1 + it * (per // SPL)
                sp.wait_ge(lo_dve[n0 % SPL], before)
                sp.wait_ge(lo_pool[n0 % SPL], before)
                if not isinstance(it, int):
                    sp.wait_ge(hi_ready, n0 - depth + 1)
            _, k, f = src.shape
            sp.dma_start(view(raw[slot], (k, f)), src).then_inc(raw_in[slot], 16)

        def split_hi(act, stage, key, size=SLAB, it=0):
            n0, per, slot, use, uses, _ = slabs[stage, key]
            act.wait_ge(raw_in[slot], 16 * (use + 1) + it * (16 * uses))
            if n0 >= SPL:
                act.wait_ge(slab_used, n0 - SPL + 1 + it * per)
            nc.scalar.activation(hi[n0 % SPL][:, 0:size], raw[slot][:, 0:size], ACT.Copy).then_inc(hi_ready, 1)

        def split_lo(eng, stage, key, size=SLAB, it=0):
            n0, per, slot, _, _, _ = slabs[stage, key]
            at = size * 5 // 8
            cols, ready = (slice(at, size), lo_pool) if eng is nc.gpsimd else (slice(0, at), lo_dve)
            eng.wait_ge(hi_ready, n0 + 1 + it * per)
            eng.tensor_tensor(lo[n0 % SPL][:, cols], raw[slot][:, cols], hi[n0 % SPL][:, cols].bitcast(F32),
                              ALU.subtract).then_inc(ready[n0 % SPL], 1)

        def slab(pe, stage, key, shape, it=0):
            n0, per = slabs[stage, key][:2]
            there = n0 // SPL + 1 + it * (per // SPL)
            pe.wait_ge(lo_dve[n0 % SPL], there)
            pe.wait_ge(lo_pool[n0 % SPL], there)
            return view(hi[n0 % SPL], shape), view(lo[n0 % SPL], shape)

        def bank(pe, stage, key, it=0):
            b, r, per = banks[stage, key][:3]
            if r:
                pe.wait_ge(bank_emptied[b], r + it * per)
            return ps[b]

        def filled(ins, stage, key):
            assert banks[stage, key][5] is None
            ins.then_inc(bank_full[banks[stage, key][0]], 1)

        def full(eng, stage, key, it=0):
            b, _, _, r, per, closing = banks[stage, key]
            if closing is None:
                eng.wait_ge(bank_full[b], r + 1 + it * per)
            elif stage == "ffn":
                eng.wait_ge(slab_used, ffn_slab(closing, it) + 1)
            else:
                n0, per = slabs[stage, closing][:2]
                eng.wait_ge(slab_used, n0 + 1 + it * per)
            return ps[b]

        def ffn_slab(kind, i):
            n = slabs["ffn_in", "g0"][0]
            if isinstance(i, int):
                return n + {"g": max(3 * i - 1, 0), "u": max(3 * i, 1), "d": min(3 * i + 4, 3 * FFI - 1)}[kind]
            return i * 3 + (n + {"g": -1, "u": 0, "d": 4}[kind])

        def emptied(ins, stage, key):
            ins.then_inc(bank_emptied[banks[stage, key][0]], 1)

        def await_emptied(eng, stage, key, it=0):
            b, r, per = banks[stage, key][:3]
            eng.wait_ge(bank_emptied[b], r + 1 + it * per)

        def product(pe, dst, lh, ll, rh, rl, first, last):
            nc.tensor.matmul(dst, lh, rh, start=first, stop=False, skip_group_check=True)
            nc.tensor.matmul(dst, lh, rl, start=False, stop=False, skip_group_check=True)
            return nc.tensor.matmul(dst, ll, rh, start=False, stop=last, skip_group_check=True)

        NORM_TILES = [range(4), range(4), range(4), range(2, 4)]

        def norm_scratch(i):
            if i == 0:
                return ([u[:, 0:2, :], u[:, 2:4, :], v[:, 0:2, :], v[:, 2:4, :]], htmpA)
            if i == 1:
                return ([yacc[:, t, :] for t in range(4)], sg)
            if i == 2:
                return ([kv[:, t, :] for t in range(4)], pexp)
            return ([None, None, xnM[:, 0, :], xnM[:, 1, :]], sge)

        def xt(i, t):
            return X[:, t, :].rearrange("p (a b) -> p a b", a=2) if i == 0 else X[:, t, :]

        def H_of(i):
            return (H1hi, H1lo) if i == 2 else (Hhi, Hlo)

        COMPRESSED = [("cq", b_, 256, b_) for b_ in range(3)] + [("ckv", b_, 512, 4 + b_) for b_ in range(2)]

        def slab_size(stage, key):
            return {"uq": 3 * 384, "cd_in": 8 * min(256, CDIN - 256 * key) if stage == "cd_in" else 0}.get(stage, SLAB)

        def unit(i):
            return i // 16, i // 2 % 8, i % 2

        def att_scale(i):
            return (64 if i < 16 else 96) ** -0.5

        def xn_block(i, t, k):
            x = norm_scratch(i)[0][t]
            return x[:, k // 4, (k % 4) * P:(k % 4 + 1) * P] if i == 0 else x[:, k * P:(k + 1) * P]

        def xn_all(i, t):
            return norm_scratch(i)[0][t]

        def columns(w, k, f0, f1):
            return w.rearrange("(k p) f -> p k f", p=P)[:, k, f0:f1]

        def expert_slabs(w):
            s = []
            for c in range(5):
                for kind in "gu":
                    for q in range(2):
                        s.append((kind, c, slice(4 * q, 4 * q + 4), slice(512 * c, 512 * c + 512)))
            s += [(kind, 5, slice(0, 8), slice(2560, 2816)) for kind in "gu"]
            s += [("d", j, slice(2 * j, 2 * j + 2), slice(0, D)) for j in range(11)]
            return s
        ES = expert_slabs(0)

        block = ctx.enter_context(nc.Block())

        @block.sync
        def _(sp):
            def ada(layer):
                for cb in range(12):
                    for h in range(2):
                        load(sp, f"ada{layer}", (cb, h),
                             columns(a["ada_w"][layer], slice(4 * h, 4 * h + 4), 512 * cb, 512 * cb + 512))

            ada(0)
            for j in range(6):
                load(sp, "ab_in", j, columns(a["ab_w_in"][0], slice(0, 8), 256 * j, 256 * j + 256))
            for h in range(2):
                for q in range(2):
                    load(sp, "ab_out", (h, q), columns(a["ab_w_out"][0], slice(4 * q, 4 * q + 4), 512 * h, 512 * h + 512))
            wg, wu, wd = (a[n][0].rearrange("(k p) f -> p k f", p=P) for n in ("ffn_w_gate", "ffn_w_up", "ffn_w_down"))

            def gate(stage, key, w, i, it=0):
                load(sp, stage, key, w[:, :, bass.ds(i * 256, 256)], it)

            def down(stage, key, i, it=0):
                load(sp, stage, key, wd[:, bass.ds(i * 2, 2), :], it)
            gate("ffn_in", "g0", wg, 0)
            gate("ffn_in", "u0", wu, 0)
            gate("ffn_in", "g1", wg, 1)
            with sp.Fori(0, 4) as it:
                for w, name in enumerate("AB"):
                    gate("ffn_loop", "u" + name, wu, it * 2 + (w + 1), it)
                    down("ffn_loop", "d" + name, it * 2 + w, it)
                    gate("ffn_loop", "g" + name, wg, it * 2 + (w + 2), it)
            gate("ffn_out", "u9", wu, 9)
            down("ffn_out", "d8", 8)
            gate("ffn_out", "g10", wg, 10)
            gate("ffn_out", "u10", wu, 10)
            down("ffn_out", "d9", 9)
            down("ffn_out", "d10", 10)
            ada(1)
            for j in range(6):
                load(sp, "cd_in", j, columns(a["cd_w_in"][0], slice(0, 8), 256 * j, min(256 * j + 256, CDIN)))
            for h in range(2):
                load(sp, "uq", h, columns(a["d_w_uq"][0], slice(0, 3), 384 * h, 384 * h + 384))
            load(sp, "ukv", 0, columns(a["d_w_ukv"][0], slice(0, 2), 0, D))
            for h in range(2):
                for q in range(2):
                    load(sp, "cd_out", (h, q), columns(a["cd_w_out"][0], slice(4 * q, 4 * q + 4), 512 * h, 512 * h + 512))
            mw = {k: a[n][0].rearrange("e (k p) f -> e p k f", p=P)
                  for k, n in (("g", "moe_w_gate"), ("u", "moe_w_up"), ("d", "moe_w_down"))}

            def expert(stage, w, e, it):
                for s, (kind, _, ks, fs) in enumerate(ES):
                    load(sp, stage, (w, s), mw[kind][bass.ds(e, 1), :, ks, fs].rearrange("e p k f -> p (e k) f"), it)
            with sp.Fori(0, NE // 2) as it:
                for w in range(2):
                    expert("moe", w, it * 2 + w, it)
            sp.wait_ge(routed, 1)
            with sp.Fori(0, OVER) as j:
                more = sp.value_load(over_i[0:1, 0, bass.ds(j, 1)], min_val=0, max_val=NE)
                with sp.If(more > 0):
                    expert("over", 0, sp.value_load(over_i[0:1, 1, bass.ds(j, 1)], min_val=0, max_val=NE - 1), j)
            for t in range(2):
                sp.wait_ge(fin_ready, t + 1)
                sp.dma_start(out[0, t * P:(t + 1) * P, :], yM[:, t, :]).then_inc(stored, 16)
            sp.wait_ge(stored, 32)

        @block.gpsimd
        def _(pool):
            def ada(layer):
                for cb in range(12):
                    if cb >= 2:
                        last = ("bc", cb - 2, 1 - layer) if (cb - 2) // 2 in (2, 5) else ("col", cb - 2)
                        full(pool, f"ada{layer}", last)
                    elif layer == 1:
                        pool.wait_ge(x_ready[1], 4)
                    pool.dma_start(mrow[4:5, cb % 2, :], a["ada_b"][layer:layer + 1, 512 * cb:512 * cb + 512]).then_inc(bias_in[cb % 2], 16)
                    for h in range(2):
                        split_lo(nc.gpsimd, f"ada{layer}", (cb, h))

            ada(0)
            for j in range(6):
                split_lo(nc.gpsimd, "ab_in", j)
            for h in range(2):
                for q in range(2):
                    split_lo(nc.gpsimd, "ab_out", (h, q))
            for key in ("g0", "u0", "g1"):
                split_lo(nc.gpsimd, "ffn_in", key)
            with pool.Fori(0, 4) as it:
                for key in ("uA", "dA", "gA", "uB", "dB", "gB"):
                    split_lo(nc.gpsimd, "ffn_loop", key, it=it)
            for key in ("u9", "d8", "g10", "u10", "d9", "d10"):
                split_lo(nc.gpsimd, "ffn_out", key)
            ada(1)
            for j in range(6):
                split_lo(nc.gpsimd, "cd_in", j, 8 * min(256, CDIN - 256 * j))
            for h in range(2):
                split_lo(nc.gpsimd, "uq", h, 3 * 384)
            split_lo(nc.gpsimd, "ukv", 0)
            for h in range(2):
                for q in range(2):
                    split_lo(nc.gpsimd, "cd_out", (h, q))

            with pool.Fori(0, NE // 2) as it:
                for w in range(2):
                    for s in range(33):
                        split_lo(nc.gpsimd, "moe", (w, s), it=it)
            pool.wait_ge(routed, 1)
            with pool.Fori(0, OVER) as j:
                more = pool.value_load(over_i[0:1, 0, bass.ds(j, 1)], min_val=0, max_val=NE)
                with pool.If(more > 0):
                    for s in range(33):
                        split_lo(nc.gpsimd, "over", (0, s), it=j)

        @block.scalar
        def _(act):
            chain = Count(act, act_chain)
            act.dma_start(crows[0:8, :], a["c"].rearrange("b (k p) -> (b k) p", p=P)).then_inc(c_in, 16)
            act.dma_start(crows[8:16, :], a["c_ctx"].rearrange("(k p) -> k p", p=P)).then_inc(c_in, 16)
            act.dma_start(crows[16:20, :], a["a_b_s"][0]).then_inc(c_in, 16)
            act.dma_start(crows[20:24, :], a["b_scale"][0].rearrange("(k p) -> k p", p=P)).then_inc(c_in, 16)
            act.dma_start(crows[24:27, :], a["d_cq_gain"][0].rearrange("(k p) -> k p", p=P)).then_inc(c_in, 16)
            act.dma_start(crows[27:29, :], a["d_ckv_gain"][0].rearrange("(k p) -> k p", p=P)).then_inc(c_in, 16)
            act.dma_start(ident[:], a["k_ident"]).then_inc(ident_in, 16)
            act.dma_start(sel[:], a["k_sel"]).then_inc(sel_in, 16)
            act.dma_start(X[:, 0:2, :], a["ctx"][0].rearrange("(t p) d -> p t d", p=P)).then_inc(x_in, 16)
            act.dma_start(X[:, 2:4, :], a["x"][0].rearrange("(t p) d -> p t d", p=P)).then_inc(x_in, 16)
            for dst, src in ((ws, a["a_w_s"][0].rearrange("g p q -> p g q")),
                             (wpool[:], a["b_w_pool"][0].rearrange("g i o -> i g o")),
                             (band[:], a["k_band"]), (vgain[:], a["a_v_gain"][0].partition_broadcast(P))):
                act.dma_start(dst, src).then_inc(ab_consts, 16)
            for dst, src in ((ropec[:], a["k_ropec"]), (roped[:], a["k_roped"]),
                             (q_gain[:], a["c_q_gain"][0].partition_broadcast(P)),
                             (k_gain[:], a["c_k_gain"][0].partition_broadcast(P))):
                act.dma_start(dst, src).then_inc(l1_in, 16)
            def splits(stage, *keys, it=0, size=SLAB):
                for key in keys:
                    split_hi(act, stage, key, size, it)

            nc.scalar.activation(cs[:], full(act, "start", "cT")[:, 0:16], ACT.Silu).then_inc(silu_c, 1)
            act.wait_ge(silu_c, 1)
            nc.scalar.activation(C4[:, :, 0:2], cs[:].rearrange("p (w k) -> p k w", w=2), ACT.Copy).then_inc(c_hi, 1)

            def ada(layer, gate_of):
                st = f"ada{layer}"

                def gate(cb):
                    for who in range(2 - layer):
                        b = full(act, st, ("bc", cb, who))
                        emptied(nc.scalar.activation(gate_of[who][:, cb // 6, (cb % 2) * 512:(cb % 2 + 1) * 512],
                                                     b[:], ACT.Copy), st, ("bc", cb, who))
                for cb in range(12):
                    splits(st, (cb, 0))
                    if cb - 2 in GATE_BLOCKS:
                        gate(cb - 2)
                    splits(st, (cb, 1))
                gate(10)
                gate(11)

            def norm(i, layer, kinds):
                tiles = NORM_TILES[i]
                ht = norm_scratch(i)[1]
                for t in tiles:
                    nc.scalar.activation(xn_all(i, t), xt(i, t), ACT.Square, accum_out=ssq[:, t, 0:1]).then_inc(sumsq[i], 1)
                act.wait_ge(meansq[i], 1)
                nc.scalar.activation(root[:, tiles[0]:4, 0:1], rstd[:, tiles[0]:4, 0:1], ACT.Sqrt).then_inc(rooted[i], 1)
                for cb in range(12):
                    if cb not in GATE_BLOCKS:
                        await_emptied(act, f"ada{layer}", ("col", cb))
                for k in range(8):
                    b = full(act, f"norm{i}", k)
                    if i < 3 and k >= 2:
                        act.wait_ge(h_ready[i], k - 1)
                    for who in ((1, 0) if i < 3 else (0,)):
                        cols = slice(256 * (1 - who), 256 * (2 - who)) if i < 3 else slice(0, 256)
                        ins = nc.scalar.activation(ht[:, k % 2, cols] if i < 3 else h2T[:, k, :], b[:, cols], ACT.Identity,
                                                   scale=modcol[layer][:, kinds + 1, k, who:who + 1],
                                                   bias=modcol[layer][:, kinds, k, who:who + 1])
                        if who:
                            chain.mark(ins)
                    emptied(ins, f"norm{i}", k)

            ada(0, gates)
            await_emptied(act, "start", "cT")
            splits("ab_in", 0, 1, 2)
            act.wait_ge(x_in, 32)
            norm(0, 0, 0)
            ahead = [("ab_in", 3), ("ab_in", 4), ("ab_in", 5), ("ab_out", (0, 0)), ("ab_out", (0, 1)), ("ab_out", (1, 0))]
            for j in range(6):
                if j < 4:
                    for t in range(NT):
                        dst = (u if j < 2 else v)[:, t, (j % 2) * 256:(j % 2 + 1) * 256]
                        emptied(nc.scalar.activation(dst, full(act, "ab_in", (j, t))[:, 0:256], ACT.Gelu), "ab_in", (j, t))
                splits(*ahead[j])
            for t in range(NT):
                await_emptied(act, "ab_in", (3, t))
                if t:
                    act.wait_ge(sumsq[4], t)
                nc.scalar.activation(vsq, v[:, t, :], ACT.Square, accum_out=ssq[:, t, 1:2]).then_inc(sumsq[4], 1)
            act.wait_ge(meansq[4], 1)
            nc.scalar.activation(root[:, :, 1:2], rstd[:, :, 1:2], ACT.Sqrt).then_inc(rooted[4], 1)
            act.wait_ge(ab_consts, 16 * 4)
            for g in range(4):
                b = full(act, "ab_yb", g)
                if g >= 2:
                    act.wait_ge(y_ready, g - 1)
                emptied(nc.scalar.activation(ybtmp[:, g % 2, :], b[:], ACT.Copy, scale=bscale_col[:, g:g + 1]), "ab_yb", g)
            for g in range(4):
                nc.scalar.activation(Hhi[:, g, :], full(act, "ab_ya", g)[:], ACT.Copy).then_inc(ya_hi, 1)
            splits("ab_out", (1, 1))
            splits("ffn_in", "g0", "u0")
            act.wait_ge(x_ready[0], 8)
            norm(1, 0, 2)
            splits("ffn_in", "g1")

            def silu(i, first=False):
                for b in range(2):
                    if not first:
                        await_emptied(act, "ffn", ("u", b), i - 1)
                    src = full(act, "ffn", ("g", b), i)
                    emptied(nc.scalar.activation(sg[:, b, :], src[:], ACT.Silu), "ffn", ("g", b))

            def ffn_step(stage, keys, i, it=0):
                splits(stage, *keys[:2], it=it)
                silu(i)
                splits(stage, keys[2], it=it)
            act.wait_ge(h_ready[1], 8)
            silu(0, first=True)
            with act.Fori(0, 4) as it:
                for w in range(2):
                    ffn_step("ffn_loop", LOOP_KEYS[w], it * 2 + (1 + w), it)
            ffn_step("ffn_out", OUT_KEYS[0], 9)
            ffn_step("ffn_out", OUT_KEYS[1], 10)
            act.wait_ge(x_ready[1], 4)
            ada(1, [gates1])
            splits("cd_in", 0, 1, 2)
            norm(2, 1, 0)
            ahead = [("cd_in", 3), ("cd_in", 4), ("cd_in", 5), ("uq", 0), ("uq", 1), ("ukv", 0)]
            for j in range(6):
                for t in CD_TILES[j]:
                    width = min(256, CDIN - 256 * j)
                    dst = Zx[:, t - 2, 256 * j:256 * j + width] if t >= 2 else Zt[:, t, ZT0[j]:ZT0[j] + width]
                    emptied(nc.scalar.activation(dst, full(act, "cd_in", (j, t))[:, 0:width], ACT.Copy), "cd_in", (j, t))
                stage, key = ahead[j]
                splits(stage, key, size=slab_size(stage, key))
            await_emptied(act, "cd_in", (5, 3))
            act.wait_ge(ssq_clear, 1)
            for a_ in range(2):
                if a_:
                    chain.wait()
                chain.mark(nc.scalar.activation(pT[:, 0, 0:384], Zx[:, a_, CQ0:CKV0], ACT.Square, accum_out=ssq[:, 2 + a_, 10:11]))
            for t in range(NT):
                src = Zx[:, t - 2, CKV0:KR0] if t >= 2 else Zt[:, t, 384:640]
                if t:
                    act.wait_ge(sumsq[5], t)
                nc.scalar.activation(pT[:, 1, 0:256], src, ACT.Square, accum_out=ssq[:, t, 11:12]).then_inc(sumsq[5], 1)
            act.wait_ge(meansq[5], 1)
            nc.scalar.activation(root[:], rstd[:], ACT.Sqrt).then_inc(rooted[5], 1)
            act.wait_ge(l1_in, 16 * 4)
            for n_, (stage, b_, cols, col) in enumerate(COMPRESSED):
                src = full(act, stage, b_)
                if n_ >= 2:
                    act.wait_ge(cqn_ready, n_ - 1)
                gain = (cq_gain if stage == "cq" else ckv_gain)[:, b_:b_ + 1]
                emptied(nc.scalar.activation(X[:, 0, (n_ % 2) * 512:(n_ % 2) * 512 + cols], src[:, 0:cols], ACT.Copy,
                                             scale=gain), stage, b_)
            for h in range(2):
                for a_ in range(2):
                    emptied(nc.scalar.activation(qd[:, a_, 384 * h:384 * h + 384], full(act, "uq", (h, a_))[:, 0:384], ACT.Copy),
                            "uq", (h, a_))
            splits("cd_out", (0, 0), (0, 1))
            for t in range(NT):
                for h in range(2):
                    emptied(nc.scalar.activation(kv[:, t, 512 * h:512 * h + 512], full(act, "ukv", (t, h))[:], ACT.Copy),
                            "ukv", (t, h))
            splits("cd_out", (1, 0))
            for h in range(8):
                emptied(nc.scalar.activation(kdT[0:64, h, :], full(act, "heads", ("kd", h))[0:64, :], ACT.Copy), "heads", ("kd", h))
            for i in range(32):
                b = full(act, "att", ("s", i))
                act.wait_ge(negmax, i + 1)
                if i >= 2:
                    full(act, "att", ("t", i - 2))
                emptied(nc.scalar.activation(pexp[:, i % 2, :], b[:], ACT.Exp, bias=rowmax[:, 1, i:i + 1], scale=att_scale(i),
                                             accum_out=rowsum[:, 0, i:i + 1]), "att", ("s", i))
            for b_ in range(4):
                nc.scalar.activation(oTh[:, 2 * b_:2 * b_ + 2, :], full(act, "oT", b_)[:], ACT.Copy).then_inc(oT_hi, 1)
            splits("cd_out", (1, 1))
            act.wait_ge(x_ready[2], 4)
            norm(3, 1, 2)
            for dst, src in ((ones[:], a["k_ones"]), (tri[:], a["k_tri"]), (slot_row[:], a["k_slot"]),
                             (expert_row[:], a["k_expert"]), (router[:], a["moe_router"][0].rearrange("(k p) e -> p k e", p=P))):
                act.dma_start(dst, src).then_inc(experts_in, 16)
            act.dma_start(fgain[:], a["final_gain"].partition_broadcast(P)).then_inc(fgain_in, 16)
            for b_ in range(4):
                nc.scalar.activation(h2h[:, b_ // 2, (b_ % 2) * 512:(b_ % 2 + 1) * 512],
                                     full(act, "route", ("back", b_))[:], ACT.Copy).then_inc(h2_hi, 1)
            act.wait_ge(logit_diff, 1)
            nc.scalar.activation(wts[:, :, 1:2], wts[:, :, 0:1], ACT.Exp).then_inc(gexp, 1)

            def gathered(stage, w, it=0):
                for h in range(2):
                    emptied(nc.scalar.activation(xgh[:, 4 * h:4 * h + 4, :], full(act, stage, ("xh", w, h), it)[:], ACT.Copy),
                            stage, ("xh", w, h))
                emptied(nc.scalar.activation(PT[:, 1 - w, :, :], full(act, stage, ("pt", w), it)[:, 0:256], ACT.Copy),
                        stage, ("pt", w))

            def silu_e(st, w, c, it):
                n_ = 512 if c < 5 else 256
                emptied(nc.scalar.activation(sge[:, c % 2, 0:n_], full(act, st, ("g", w, c), it)[:, 0:n_], ACT.Silu),
                        st, ("g", w, c))

            def act_hi(st, w, c, it):
                n_ = 4 if c < 5 else 2
                nc.scalar.activation(aTh[:, 4 * c:4 * c + n_, :], full(act, st, ("t", w, c), it)[:, 0:n_ * P],
                                     ACT.Copy).then_inc(hi_out[st == "over"], 1)

            def out_hi(st, w, it):
                for h in range(2):
                    nc.scalar.activation(yeh[:, h, :], full(act, st, ("d", w, h), it)[:], ACT.Copy).then_inc(hi_out[st == "over"], 1)

            def expert(st, w, it):
                for s in range(33):
                    split_hi(act, st, (w, s), it=it)
                    if w == 1 and s == 1:
                        out_hi(st, 0, it)
                    if s % 4 == 0 and 4 <= s <= 20:
                        silu_e(st, w, s // 4 - 1, it)
                    if s == 22:
                        silu_e(st, w, 5, it)
                    if s in (10, 14, 18, 22):
                        act_hi(st, w, (s - 10) // 4, it)
                    if s == 23:
                        act_hi(st, w, 4, it)
                    if s == 24:
                        if st == "moe":
                            gathered(st, w, it)
                        act_hi(st, w, 5, it)
            gathered("first", 1)
            with act.Fori(0, NE // 2) as it:
                expert("moe", 0, it)
                expert("moe", 1, it)
                out_hi("moe", 1, it)
            act.wait_ge(routed, 1)
            with act.Fori(0, OVER) as j:
                more = act.value_load(over_i[0:1, 0, bass.ds(j, 1)], min_val=0, max_val=NE)
                with act.If(more > 0):
                    gathered("over", 1, j)
                    expert("over", 0, j)
                    out_hi("over", 0, j)
            for t in range(2):
                act.wait_ge(y_done, t + 1)
                nc.scalar.activation(yM[:, t, :], X[:, 2 + t, :], ACT.Square, accum_out=ssq[:, t, 0:1]).then_inc(sumsq[6], 1)
            act.wait_ge(meansq[6], 1)
            nc.scalar.activation(root[:, 0:2, 0:1], rstd[:, 0:2, 0:1], ACT.Sqrt).then_inc(rooted[6], 1)

        @block.vector
        def _(dve):
            chain = Count(dve, dve_chain)
            V = nc.vector

            def splits(stage, *keys, it=0, size=SLAB):
                for key in keys:
                    split_lo(V, stage, key, size, it)

            def hi_lo(dst_hi, dst_lo, src, ready):
                chain.mark(V.tensor_copy(dst_hi, src))
                chain.wait()
                V.tensor_tensor(dst_lo, src, dst_hi.bitcast(F32), ALU.subtract).then_inc(ready, 1)

            def inverse_root(i, parts):
                for p_, (dst, src, n_) in enumerate(parts):
                    ins = V.tensor_scalar(dst, src, 1.0 / n_, EPS, ALU.mult, ALU.add)
                    if p_ < len(parts) - 1:
                        chain.mark(ins)
                ins.then_inc(meansq[i], 1)
                dve.wait_ge(rooted[i], 1)

            def norm(i):
                tiles = NORM_TILES[i]
                ht = norm_scratch(i)[1]
                dve.wait_ge(sumsq[i], len(tiles))
                cols = (slice(None), slice(tiles[0], 4), slice(0, 1))
                inverse_root(i, [(rstd[cols], ssq[cols], D)])
                chain.mark(V.reciprocal(rstd[cols], root[cols]))
                chain.wait()
                for t in tiles:
                    V.tensor_scalar(xn_all(i, t), xt(i, t), rstd[:, t, 0:1], None, ALU.mult).then_inc(xn_ready[i], 1)
                if i < 3:
                    for k in range(8):
                        await_emptied(dve, f"norm{i}", k)
                        hi_lo(H_of(i)[0][:, k, :], H_of(i)[1][:, k, :], ht[:, k % 2, :], h_ready[i])

            def residual(stage, key, n_, t, gate, tmp, ready):
                h = key[0]
                cols = slice(512 * h, 512 * h + 512)
                b = full(dve, stage, key)
                if n_ >= 2:
                    dve.wait_ge(ready, n_ - 1)
                emptied(V.tensor_tensor(tmp, b[:], gate[:, cols], ALU.mult), stage, key)
                await_emptied(dve, stage, key)
                V.tensor_tensor(X[:, t, cols], X[:, t, cols], tmp, ALU.add).then_inc(ready, 1)

            dve.wait_ge(silu_c, 1)
            emptied(V.tensor_copy(pcols[:], full(dve, "start", "cT")[:, 16:29]), "start", "cT")
            dve.wait_ge(c_hi, 1)
            V.tensor_tensor(C4[:, :, 2:4], cs[:].rearrange("p (w k) -> p k w", w=2), C4[:, :, 0:2].bitcast(F32),
                            ALU.subtract).then_inc(c_lo, 1)
            emptied(V.tensor_copy(wsT[:], full(dve, "start", "wsT")[:]), "start", "wsT")

            def ada(layer):
                st = f"ada{layer}"

                def row(cb):
                    b = full(dve, st, ("m", cb))
                    if cb >= 2:
                        full(dve, st, ("bc", cb - 2, 1 - layer) if cb - 2 in GATE_BLOCKS else ("col", cb - 2))
                    elif layer == 1:
                        full(dve, "ada0", ("bc", 10 + cb, 1))
                    emptied(V.tensor_copy(mrow[0:4, cb % 2, :], b[0:4, :]), st, ("m", cb))

                def col(cb):
                    kind = KIND[cb // 2]
                    b = full(dve, st, ("col", cb))[:, 0:8].rearrange("p (j w) -> p j w", w=2)
                    emptied(V.tensor_scalar(modcol[layer][:, kind, (cb % 2) * 4:(cb % 2 + 1) * 4, :], b, float(kind % 2),
                                            None, ALU.add), st, ("col", cb))
                for cb in range(12):
                    splits(st, (cb, 0))
                    if cb >= 1:
                        row(cb - 1)
                    splits(st, (cb, 1))
                    if cb >= 2 and cb - 2 not in GATE_BLOCKS:
                        col(cb - 2)
                row(11)

            ada(0)
            splits("ab_in", 0, 1, 2)
            norm(0)
            await_emptied(dve, "start", "cT")
            dve.wait_ge(ab_consts, 16 * 4)
            ahead = [("ab_in", 3), ("ab_in", 4), ("ab_in", 5), ("ab_out", (0, 0)), ("ab_out", (0, 1)), ("ab_out", (1, 0))]
            for j in range(6):
                if j < 4:
                    await_emptied(dve, "ab_in", (j, 3))
                else:
                    for t in range(NT):
                        b = full(dve, "ab_in", (j, t))
                        emptied(V.tensor_copy(zp[:, t, (j - 4) * 256:(j - 3) * 256], b[:, 0:256]), "ab_in", (j, t))
                splits(*ahead[j])
            dve.wait_ge(sumsq[4], NT)
            inverse_root(4, [(rstd[:, :, 1:2], ssq[:, :, 1:2], AW)])
            chain.mark(V.reciprocal(rstd[:, :, 1:2], root[:, :, 1:2]))
            chain.wait()
            for t in range(NT):
                V.scalar_tensor_tensor(out=v[:, t, :], in0=v[:, t, :], scalar=rstd[:, t, 1:2], in1=vgain[:],
                                       op0=ALU.mult, op1=ALU.mult).then_inc(v_ready, 1)
            for t in range(NT):
                b = full(dve, "ab_s", t)
                for g in range(4):
                    cols = slice(g * P, (g + 1) * P)
                    ins = V.scalar_tensor_tensor(out=u[:, t, cols], in0=b[:, cols], scalar=bs_col[:, g:g + 1], in1=u[:, t, cols],
                                                 op0=ALU.add, op1=ALU.mult)
                    if g < 3:
                        chain.mark(ins)
                emptied(ins, "ab_s", t)

            def pooled(g):
                b = full(dve, "ab_pool", g)
                if g >= 2:
                    full(dve, "ab_yb", g - 2)
                emptied(V.tensor_copy(pooledT[:, g % 2, :], b[:]), "ab_pool", g)

            def yb(g):
                await_emptied(dve, "ab_yb", g)
                hi_lo(Hhi[:, 4 + g, :], Hlo[:, 4 + g, :], ybtmp[:, g % 2, :], y_ready)
            pooled(0)
            for g in range(4):
                if g < 3:
                    pooled(g + 1)
                yb(g)
            for g in range(4):
                b = full(dve, "ab_ya", g)
                dve.wait_ge(ya_hi, g + 1)
                emptied(V.tensor_tensor(Hlo[:, g, :], b[:], Hhi[:, g, :].bitcast(F32), ALU.subtract), "ab_ya", g)
            splits("ab_out", (1, 1))
            for t in range(NT):
                residual("ab_out", (0, t), t, t, gates[int(t < 2)][:, 0, :], u[:, t % 2, :], x_ready[0])
            splits("ffn_in", "g0", "u0")
            for t in range(NT):
                residual("ab_out", (1, t), 4 + t, t, gates[int(t < 2)][:, 0, :], u[:, t % 2, :], x_ready[0])
            norm(1)
            splits("ffn_in", "g1")

            def hidden(i, parity):
                for b_ in range(2):
                    await_emptied(dve, "ffn", ("g", b_), i)
                    b = full(dve, "ffn", ("u", b_), i)
                    emptied(V.tensor_tensor(am[:, b_, :], b[:], sg[:, b_, :], ALU.mult), "ffn", ("u", b_))
                for b_ in range(2):
                    await_emptied(dve, "ffn", ("u", b_), i)
                    ins = V.tensor_copy(acth[:, parity, b_, :], am[:, b_, :])
                    chain.mark(ins)
                chain.wait()
                for b_ in range(2):
                    V.tensor_tensor(actl[:, parity, b_, :], am[:, b_, :], acth[:, parity, b_, :].bitcast(F32),
                                    ALU.subtract).then_inc(ff_ready, 1)

            def add_down(i, outs, first=False):
                for o in outs:
                    t, h = o % 4, o // 4
                    b = full(dve, "ffn", ("d", o), i)
                    y = yacc[:, t, 512 * h:512 * h + 512]
                    if first:
                        emptied(V.tensor_copy(y, b[:]), "ffn", ("d", o))
                    else:
                        emptied(V.tensor_tensor(y, y, b[:], ALU.add), "ffn", ("d", o))

            def ffn_step(stage, keys, i, parity, it=0, first=False):
                splits(stage, *keys[:2], it=it)
                hidden(i, parity)
                add_down(i - 1, range(4), first)
                splits(stage, keys[2], it=it)
                add_down(i - 1, range(4, 8), first)
            hidden(0, 0)
            dve.wait_ge(ff_ready, 2)
            chain.mark(V.memset(yacc[:], 0.0))
            chain.wait()
            with dve.Fori(0, 4) as it:
                chain.enter(it, 4)
                for w in range(2):
                    ffn_step("ffn_loop", LOOP_KEYS[w], it * 2 + (1 + w), 1 - w, it)
                chain.leave(4)
            ffn_step("ffn_out", OUT_KEYS[0], 9, 1)
            ffn_step("ffn_out", OUT_KEYS[1], 10, 0)
            add_down(10, range(8))
            for t in range(NT):
                await_emptied(dve, "ffn", ("d", 4 + t), 10)
                chain.mark(V.tensor_tensor(yacc[:, t, :], yacc[:, t, :], gates[int(t < 2)][:, 1, :], ALU.mult))
            chain.wait()
            for t in range(NT):
                V.tensor_tensor(X[:, t, :], X[:, t, :], yacc[:, t, :], ALU.add).then_inc(x_ready[1], 1)
            ada(1)
            splits("cd_in", 0, 1, 2)
            norm(2)
            V.memset(ssq[:], 1.0).then_inc(ssq_clear, 1)
            ahead = [("cd_in", 3), ("cd_in", 4), ("cd_in", 5), ("uq", 0), ("uq", 1), ("ukv", 0)]
            for j in range(6):
                await_emptied(dve, "cd_in", (j, 3))
                stage, key = ahead[j]
                splits(stage, key, size=slab_size(stage, key))
            dve.wait_ge(l1_in, 16 * 4)
            dve.wait_ge(ssq_clear, 1)

            def heads(x, n_, d=64):
                return x.rearrange("p (h d) -> p h d", h=n_)
            sq = pexp[:].rearrange("p a b -> p (a b)")
            for t in range(NT):
                src, h0 = (Zx[:, t - 2, 0:640], 0) if t >= 2 else (Zt[:, t, 0:128], 8)
                n_ = (10 - h0) * 64
                chain.wait()
                chain.mark(V.tensor_tensor(sq[:, 0:n_], src, src, ALU.mult))
                chain.wait()
                chain.mark(V.tensor_reduce(ssq[:, t, h0:10], heads(sq[:, 0:n_], 10 - h0), AX, ALU.add))
            dve.wait_ge(sumsq[5], NT)
            chain.wait()
            inverse_root(5, [(rstd[:, :, 0:10], ssq[:, :, 0:10], 64), (rstd[:, :, 10:11], ssq[:, :, 10:11], 384),
                             (rstd[:, :, 11:12], ssq[:, :, 11:12], 256)])
            chain.mark(V.reciprocal(rstd[:], root[:]))
            chain.wait()
            for a_ in range(2):
                V.tensor_scalar(Zx[:, a_, CQ0:CKV0], Zx[:, a_, CQ0:CKV0], rstd[:, 2 + a_, 10:11], None, ALU.mult).then_inc(cn_ready, 1)
            for t in range(NT):
                x = Zx[:, t - 2, CKV0:KR0] if t >= 2 else Zt[:, t, 384:640]
                V.tensor_scalar(x, x, rstd[:, t, 11:12], None, ALU.mult).then_inc(cn_ready, 1)
            for n_, (stage, b_, cols, col) in enumerate(COMPRESSED):
                await_emptied(dve, stage, b_)
                hi_lo(H1hi[:, col, 0:cols], H1lo[:, col, 0:cols], X[:, 0, (n_ % 2) * 512:(n_ % 2) * 512 + cols], cqn_ready)

            def rope(x, tmp, table, a_, n_, half):
                s = table[:, a_, 1, :].unsqueeze(1).to_broadcast([P, n_, 2 * half])
                c = table[:, a_, 0, :].unsqueeze(1).to_broadcast([P, n_, 2 * half])
                chain.wait()
                chain.mark(V.tensor_tensor(tmp[:, :, 0:half], x[:, :, half:2 * half], s[:, :, 0:half], ALU.mult))
                chain.mark(V.tensor_tensor(tmp[:, :, half:2 * half], x[:, :, 0:half], s[:, :, half:2 * half], ALU.mult))
                chain.wait()
                chain.mark(V.tensor_tensor(x, x, c, ALU.mult))
                chain.wait()
            for t in range(NT):
                if t < 2:
                    k_ = heads(Zt[:, t, 0:128], 2)
                else:
                    x10 = heads(Zx[:, t - 2, 0:640], 10)
                    q_, k_ = x10[:, 0:8, :], x10[:, 8:10, :]
                    chain.mark(V.tensor_tensor(q_, q_, rstd[:, t, 0:8].unsqueeze(2).to_broadcast([P, 8, 64]), ALU.mult))
                    chain.wait()
                    chain.mark(V.tensor_tensor(q_, q_, q_gain[:].unsqueeze(1).to_broadcast([P, 8, 64]), ALU.mult))
                chain.mark(V.tensor_tensor(k_, k_, rstd[:, t, 8:10].unsqueeze(2).to_broadcast([P, 2, 64]), ALU.mult))
                chain.wait()
                ins = V.tensor_tensor(k_, k_, k_gain[:].unsqueeze(1).to_broadcast([P, 2, 64]), ALU.mult)
                if t < 2:
                    ins.then_inc(qk_ready, 1)
                    continue
                chain.mark(ins)
                tmp = heads(sq[:, 0:640], 10)
                rope(x10, tmp, ropec, t - 2, 10, 32)
                chain.mark(V.tensor_tensor(tmp, tmp, x10, ALU.add))
                chain.wait()
                chain.mark(V.tensor_copy(Zx[:, t - 2, 0:512].rearrange("p (j g d) -> p g j d", j=4, g=2),
                                         sq[:, 0:512].rearrange("p (g j d) -> p g j d", g=2, j=4)))
                V.tensor_copy(Zx[:, t - 2, 512:640], sq[:, 512:640]).then_inc(qk_ready, 1)
                kr = Zx[:, t - 2, KR0:CDIN].unsqueeze(1)
                dve.wait_ge(qk_ready, t + 1)
                tmp = sq[:, 640:672].unsqueeze(1)
                rope(kr, tmp, roped, t - 2, 1, 16)
                V.tensor_tensor(kr, kr, tmp, ALU.add).then_inc(kr_ready, 1)
            splits("cd_out", (0, 0), (0, 1))
            for a_ in range(2):
                for h in range(2):
                    await_emptied(dve, "uq", (h, a_))
                x = qd[:, a_, :].rearrange("p (h d) -> p h d", h=8)[:, :, 64:96]
                tmp = sq[:, 0:256].rearrange("p (h d) -> p h d", h=8)
                rope(x, tmp, roped, a_, 8, 16)
                V.tensor_tensor(x, x, tmp, ALU.add).then_inc(rope_ready, 1)
                dve.wait_ge(rope_ready, a_ + 1)
            splits("cd_out", (1, 0))
            emptied(V.tensor_copy(kcT[:], full(dve, "heads", "kc")[:]), "heads", "kc")
            for i in range(2):
                b = full(dve, "heads", ("qc", i))
                emptied(V.tensor_copy(qcT[:, 2 * i:2 * i + 2, :], b[:].rearrange("p (j t) -> p j t", j=2)), "heads", ("qc", i))
            b = full(dve, "heads", "kr")
            emptied(V.tensor_copy(kdT[64:96, :, :], b[0:32, :].unsqueeze(1).to_broadcast([32, 8, 512])), "heads", "kr")
            for i in range(4):
                b = full(dve, "heads", ("qd", i))
                emptied(V.tensor_copy(qdT[0:96, 2 * i:2 * i + 2, :], b[0:96, :].rearrange("p (j t) -> p j t", j=2)), "heads", ("qd", i))

            for i in range(34):
                if i < 32:
                    b = full(dve, "att", ("s", i))
                    chain.mark(V.reduce_max(rowmax[:, 0, i:i + 1], b[:], AX))
                    chain.wait()
                    V.tensor_scalar(rowmax[:, 1, i:i + 1], rowmax[:, 0, i:i + 1], -att_scale(i), None, ALU.mult).then_inc(negmax, 1)
                if 2 <= i:
                    br, h, a_ = unit(i - 2)
                    await_emptied(dve, "att", ("s", i - 2))
                    chain.mark(V.reciprocal(rowsum[:, 1, i - 2:i - 1], rowsum[:, 0, i - 2:i - 1]))
                    chain.wait()
                    b = full(dve, "att", ("o", i - 2))
                    c0 = br * 512 + h * 64
                    emptied(V.tensor_scalar(X[:, a_, c0:c0 + 64], b[:, 0:64], rowsum[:, 1, i - 2:i - 1], None, ALU.mult),
                            "att", ("o", i - 2))
                if 1 <= i < 33:
                    b = full(dve, "att", ("t", i - 1))
                    if i >= 3:
                        full(dve, "att", ("o", i - 3))
                    emptied(V.tensor_copy(pT[:, (i - 1) % 2, :], b[:]), "att", ("t", i - 1))
            for b_ in range(4):
                b = full(dve, "oT", b_)
                dve.wait_ge(oT_hi, b_ + 1)
                emptied(V.tensor_tensor(oTl[:, 2 * b_:2 * b_ + 2, :], b[:].rearrange("p (j t) -> p j t", j=2),
                                        oTh[:, 2 * b_:2 * b_ + 2, :].bitcast(F32), ALU.subtract), "oT", b_)
            splits("cd_out", (1, 1))
            for h in range(2):
                for a_ in range(2):
                    residual("cd_out", (h, a_), 2 * h + a_, 2 + a_, gates1[:, 0, :], pexp[:, a_, :], x_ready[2])
            norm(3)
            chain.mark(V.memset(yM, 0.0))
            chain.mark(V.memset(posn[:], -1.0))
            chain.wait()
            for b_ in range(4):
                b = full(dve, "route", ("back", b_))
                dve.wait_ge(h2_hi, b_ + 1)
                cols = slice((b_ % 2) * 512, (b_ % 2 + 1) * 512)
                emptied(V.tensor_tensor(h2l[:, b_ // 2, cols], b[:], h2h[:, b_ // 2, cols].bitcast(F32), ALU.subtract),
                        "route", ("back", b_))
            emptied(V.tensor_copy(logits[:], full(dve, "route", "logits")[:, 0:16].rearrange("p (t e) -> p t e", t=2)), "route", "logits")
            await_emptied(dve, "route", "logits")
            dve.wait_ge(experts_in, 16 * 5)
            for t in range(2):
                chain.mark(V.max(top[:, t, :], logits[:, t, :]))
                chain.wait()
                chain.mark(V.max_index(topi[:, t, :], top[:, t, :], logits[:, t, :]))
                chain.wait()
                chain.mark(V.tensor_copy(topf[:, t, :], topi[:, t, :]))
                chain.wait()
                for j in range(2):
                    chain.mark(V.tensor_scalar(pick[:, t, j, :], expert_row[:], topf[:, t, j:j + 1], None, ALU.is_equal))
                chain.wait()
                V.tensor_tensor(chosen[:, t, :], pick[:, t, 0, :], pick[:, t, 1, :], ALU.add).then_inc(chosen_ready, 1)
            V.tensor_tensor(wts[:, :, 0:1], top[:, :, 1:2], top[:, :, 0:1], ALU.subtract).then_inc(logit_diff, 1)
            dve.wait_ge(gexp, 1)
            chain.mark(V.tensor_scalar(wts[:, :, 2:3], wts[:, :, 1:2], 1.0, None, ALU.add))
            chain.wait()
            chain.mark(V.reciprocal(wts[:, :, 2:3], wts[:, :, 2:3]))
            chain.wait()
            chain.mark(V.tensor_tensor(wts[:, :, 3:4], wts[:, :, 1:2], wts[:, :, 2:3], ALU.mult))
            chain.wait()
            for t in range(2):
                chain.mark(V.tensor_scalar(gate_e[:, t, :], pick[:, t, 0, :], wts[:, t, 2:3], None, ALU.mult))
                chain.wait()
                chain.mark(V.scalar_tensor_tensor(out=gate_e[:, t, :], in0=pick[:, t, 1, :], scalar=wts[:, t, 3:4],
                                                  in1=gate_e[:, t, :], op0=ALU.mult, op1=ALU.add))
            b = full(dve, "route", "cum")
            dve.wait_ge(chosen_ready, 2)
            chain.mark(V.tensor_tensor(posn[:, :, 0:NE], b[:, 0:16].rearrange("p (t e) -> p t e", t=2), chosen[:], ALU.mult))
            chain.wait()
            chain.mark(V.tensor_scalar(posn[:, :, 0:NE], posn[:, :, 0:NE], -1.0, None, ALU.add))
            emptied(V.tensor_scalar(over[:, 0, :], b[:, 16:24], CAP + 0.5, None, ALU.is_gt), "route", "cum")
            chain.mark(V.tensor_scalar(over[:, 1, :], expert_row[:], -1.0, float(NE), ALU.mult, ALU.add))
            chain.wait()
            await_emptied(dve, "route", "cum")
            chain.mark(V.tensor_tensor(over[:, 0, :], over[:, 0, :], over[:, 1, :], ALU.mult))
            chain.wait()
            chain.mark(V.max(over[:, 2, :], over[:, 0, :]))
            chain.wait()
            chain.mark(V.tensor_scalar(over[:, 1, :], over[:, 2, :], -1.0, float(NE), ALU.mult, ALU.add))
            chain.wait()
            chain.mark(V.tensor_scalar(over_i[:, 1, :], over[:, 1, :], float(NE - 1), None, ALU.min))
            V.tensor_copy(over_i[:, 0, :], over[:, 2, :]).then_inc(routed, 1)

            def place(r, par, e):
                for t in range(2):
                    V.tensor_scalar(Pm[:, par, t, :], slot_row[:, r * SLOTS:(r + 1) * SLOTS], posn[:, t, bass.ds(e, 1)], None,
                                    ALU.is_equal).then_inc(p_ready[r], 1)

            def gathered_lo(stage, w, it=0):
                for h in range(2):
                    emptied(V.tensor_copy(xgl[:, 4 * h:4 * h + 4, :], full(dve, stage, ("xl", w, h), it)[:]
                                          .rearrange("p (k s) -> p k s", k=4)), stage, ("xl", w, h))

            def act_e(st, w, c, it):
                n_ = 512 if c < 5 else 256
                await_emptied(dve, st, ("g", w, c), it)
                b = full(dve, st, ("u", w, c), it)
                emptied(V.tensor_tensor(ame[:, c % 2, 0:n_], b[:, 0:n_], sge[:, c % 2, 0:n_], ALU.mult), st, ("u", w, c))

            def hi_there(st, i, it):
                dve.wait_ge(hi_out[st == "over"], it * (8 if st == "over" else 16) + (i + 1))

            def act_lo(st, w, c, it):
                n_ = 4 if c < 5 else 2
                b = full(dve, st, ("t", w, c), it)
                hi_there(st, 8 * w + c, it)
                emptied(V.tensor_tensor(aTl[:, 4 * c:4 * c + n_, :], b[:, 0:n_ * P].rearrange("p (k s) -> p k s", k=n_),
                                        aTh[:, 4 * c:4 * c + n_, :].bitcast(F32), ALU.subtract), st, ("t", w, c))

            def out_lo(st, w, it):
                for h in range(2):
                    b = full(dve, st, ("d", w, h), it)
                    hi_there(st, 8 * w + 6 + h, it)
                    emptied(V.tensor_tensor(yel[:, h, :], b[:], yeh[:, h, :].bitcast(F32), ALU.subtract), st, ("d", w, h))

            def add_out(st, w, e, it):
                for o in range(4):
                    t, h = o // 2, o % 2
                    b = full(dve, st, ("y", w, o), it)
                    y = yM[:, t, 512 * h:512 * h + 512]
                    emptied(V.scalar_tensor_tensor(out=y, in0=b[:], scalar=gate_e[:, t, bass.ds(e, 1)], in1=y,
                                                   op0=ALU.mult, op1=ALU.add), st, ("y", w, o))

            def expert(st, w, it):
                for s in range(33):
                    splits(st, (w, s), it=it)
                    if w == 1 and s == 1:
                        out_lo(st, 0, it)
                    if w == 1 and s == 5:
                        add_out(st, 0, it * 2, it)
                    if s in (6, 10, 14, 18, 22):
                        act_e(st, w, (s - 6) // 4, it)
                    if s in (10, 14, 18, 22):
                        act_lo(st, w, (s - 10) // 4, it)
                    if s == 12 and st == "moe":
                        place(0, 1 - w, it * 2 + (w + 1))
                    if s == 23:
                        act_e(st, w, 5, it)
                        act_lo(st, w, 4, it)
                    if s == 24:
                        if st == "moe":
                            gathered_lo(st, w, it)
                        act_lo(st, w, 5, it)
            place(0, 0, 0)
            gathered_lo("first", 1)
            with dve.Fori(0, NE // 2) as it:
                expert("moe", 0, it)
                expert("moe", 1, it)
                out_lo("moe", 1, it)
                add_out("moe", 1, it * 2 + 1, it)
            for o in (2, 3):
                await_emptied(dve, "moe", ("y", 1, o), NE // 2 - 1)
            dve.wait_ge(routed, 1)
            V.tensor_copy(over[:, 0, 0:1], over[:, 2, 0:1]).then_inc(summed, 1)
            with dve.Fori(0, OVER) as j:
                more = dve.value_load(over_i[0:1, 0, bass.ds(j, 1)], min_val=0, max_val=NE)
                with dve.If(more > 0):
                    e = dve.value_load(over_i[0:1, 1, bass.ds(j, 1)], min_val=0, max_val=NE - 1)
                    dve.wait_ge(summed, j + 1)
                    place(1, 0, e)
                    gathered_lo("over", 1, j)
                    expert("over", 0, j)
                    out_lo("over", 0, j)
                    add_out("over", 0, e, j)
                    for o in (2, 3):
                        await_emptied(dve, "over", ("y", 0, o), j)
                    V.tensor_copy(over[:, 0, 0:1], over[:, 2, 0:1]).then_inc(summed, 1)
            dve.wait_ge(fgain_in, 16)
            for t in range(2):
                chain.mark(V.tensor_tensor(yM[:, t, :], yM[:, t, :], gates1[:, 1, :], ALU.mult))
            chain.wait()
            for t in range(2):
                V.tensor_tensor(X[:, 2 + t, :], X[:, 2 + t, :], yM[:, t, :], ALU.add).then_inc(y_done, 1)
            dve.wait_ge(sumsq[6], 2)
            inverse_root(6, [(rstd[:, 0:2, 0:1], ssq[:, 0:2, 0:1], D)])
            chain.mark(V.reciprocal(rstd[:, 0:2, 0:1], root[:, 0:2, 0:1]))
            chain.wait()
            for t in range(2):
                V.scalar_tensor_tensor(out=yM[:, t, :], in0=X[:, 2 + t, :], scalar=rstd[:, t, 0:1], in1=fgain[:],
                                       op0=ALU.mult, op1=ALU.mult).then_inc(fin_ready, 1)

        @block.tensor
        def _(pe):
            T = nc.tensor

            def used(ins):
                ins.then_inc(slab_used, 1)

            def ada(layer):
                st = f"ada{layer}"

                def columns_of(cb):
                    await_emptied(pe, st, ("m", cb))
                    pe.wait_ge(bias_in[cb % 2], 16 * (6 * layer + cb // 2 + 1))
                    row = mrow[0:5, cb % 2, :]
                    if cb in GATE_BLOCKS:
                        for who in range(2 - layer):
                            filled(T.matmul(bank(pe, st, ("bc", cb, who))[:], sel[:, who, :], row, start=True, stop=True),
                                   st, ("bc", cb, who))
                        return
                    b = bank(pe, st, ("col", cb))
                    for j in range(4):
                        ins = T.matmul(b[:, 2 * j:2 * j + 2], row[:, j * P:(j + 1) * P], sel[:, :, 0], start=True, stop=True)
                    filled(ins, st, ("col", cb))
                for cb in range(12):
                    b = bank(pe, st, ("m", cb))
                    for h in range(2):
                        wh, wl = slab(pe, st, (cb, h), (4, 512))
                        for k in range(4):
                            T.matmul(b[0:4, :], C4[:, 4 * h + k, :], wh[:, k, :], start=(h == 0 and k == 0), stop=False)
                            ins = T.matmul(b[0:4, :], C4[:, 4 * h + k, :], wl[:, k, :], start=False, stop=(h == 1 and k == 3))
                        used(ins)
                    if cb >= 1:
                        columns_of(cb - 1)
                columns_of(11)

            def norm(i):
                tiles = NORM_TILES[i]
                pe.wait_ge(xn_ready[i], len(tiles))
                for k in range(8):
                    b = bank(pe, f"norm{i}", k)
                    for n_, t in enumerate(tiles):
                        ins = T.transpose(b[:, n_ * P:(n_ + 1) * P], xn_block(i, t, k), ident[:])
                    filled(ins, f"norm{i}", k)

            def project(stage, keys, blocks, tiles, left, bank_of):
                k0 = 0
                for s_, (key, width) in enumerate(keys):
                    wh, wl = slab(pe, stage, key, (blocks, width))
                    for t in tiles:
                        b = bank(pe, stage, bank_of(t)) if s_ == 0 else ps[banks[stage, bank_of(t)][0]]
                        for k in range(blocks):
                            lh, ll = left(k0 + k, t)
                            ins = product(pe, b[:, 0:width], lh, ll, wh[:, k, :], wl[:, k, :], s_ == 0 and k == 0,
                                          s_ == len(keys) - 1 and k == blocks - 1)
                        if s_ == len(keys) - 1 and t != tiles[-1]:
                            filled(ins, stage, bank_of(t))
                    used(ins)
                    k0 += blocks

            def tok(hh, hl):
                return lambda k, t: (hh[:, k, t * P:(t + 1) * P], hl[:, k, t * P:(t + 1) * P])

            pe.wait_ge(ident_in, 16)
            pe.wait_ge(c_in, 16 * 6)
            filled(T.transpose(bank(pe, "start", "cT")[:, 0:29], crows[:], ident[0:29, 0:29]), "start", "cT")
            pe.wait_ge(ab_consts, 16 * 4)
            b = bank(pe, "start", "wsT")
            for g in range(4):
                ins = T.transpose(b[:, g * P:(g + 1) * P], ws[:, g, :], ident[:])
            filled(ins, "start", "wsT")
            pe.wait_ge(c_lo, 1)
            pe.wait_ge(sel_in, 16)
            ada(0)
            norm(0)
            pe.wait_ge(h_ready[0], 8)
            for j in range(6):
                project("ab_in", [(j, 256)], 8, range(4), tok(Hhi, Hlo), lambda t: (j, t))
            for t in range(NT):
                pe.wait_ge(v_ready, t + 1)
                b = bank(pe, "ab_s", t)
                for g in range(4):
                    ins = T.matmul(b[:, g * P:(g + 1) * P], wsT[:, g, :], v[:, t, g * P:(g + 1) * P], start=True, stop=True)
                filled(ins, "ab_s", t)

            def pool(g):
                await_emptied(pe, "ab_in", (4 + g // 2, 3))
                b = bank(pe, "ab_pool", g)
                for s_ in range(2):
                    for a_ in range(2):
                        c0 = 256 * s_ + 112 * a_
                        ins = T.matmul(b[:, c0:c0 + 144], zp[:, 2 * s_ + a_, g * P:(g + 1) * P], band[:, g, a_, :],
                                       start=(s_ == 0 and a_ == 0), stop=(s_ == 1 and a_ == 1), skip_group_check=True)
                filled(ins, "ab_pool", g)

            def yb(g):
                await_emptied(pe, "ab_pool", g)
                filled(T.matmul(bank(pe, "ab_yb", g)[:], wpool[:, g, :], pooledT[:, g % 2, :], start=True, stop=True), "ab_yb", g)
            pool(0)
            for g in range(4):
                if g < 3:
                    pool(g + 1)
                yb(g)
            for g in range(4):
                b = bank(pe, "ab_ya", g)
                for t in range(NT):
                    await_emptied(pe, "ab_s", t)
                    ins = T.transpose(b[:, t * P:(t + 1) * P], u[:, t, g * P:(g + 1) * P], ident[:])
                filled(ins, "ab_ya", g)
            pe.wait_ge(y_ready, 4)
            for g in range(4):
                await_emptied(pe, "ab_ya", g)
            for h in range(2):
                project("ab_out", [((h, 0), 512), ((h, 1), 512)], 4, range(4), tok(Hhi, Hlo), lambda t: (h, t))
            norm(1)
            pe.wait_ge(h_ready[1], 8)

            def hidden(kind, stage, key, i, it=0):
                wh, wl = slab(pe, stage, key, (8, 256), it)
                for b_ in range(2):
                    b = bank(pe, "ffn", (kind, b_), i)
                    for k in range(KD):
                        cols = slice(b_ * P, (b_ + 1) * P)
                        ins = product(pe, b[:], wh[:, k, cols], wl[:, k, cols], Hhi[:, k, :], Hlo[:, k, :], k == 0, k == KD - 1)
                    if b_ == 0:
                        filled(ins, "ffn", (kind, b_))
                used(ins)

            def down(stage, key, i, parity, it=0):
                pe.wait_ge(ff_ready, i * 2 + 2)
                wh, wl = slab(pe, stage, key, (2, D), it)
                for o in range(8):
                    t, h = o % 4, o // 4
                    b = bank(pe, "ffn", ("d", o), i)
                    for k in range(2):
                        cols, toks = slice(512 * h, 512 * h + 512), slice(t * P, (t + 1) * P)
                        ins = product(pe, b[:], acth[:, parity, k, toks], actl[:, parity, k, toks], wh[:, k, cols],
                                      wl[:, k, cols], k == 0, k == 1)
                    if o < 7:
                        filled(ins, "ffn", ("d", o))
                used(ins)
            hidden("g", "ffn_in", "g0", 0)
            hidden("u", "ffn_in", "u0", 0)
            hidden("g", "ffn_in", "g1", 1)
            with pe.Fori(0, 4) as it:
                for w in range(2):
                    ku, kd, kg = LOOP_KEYS[w]
                    hidden("u", "ffn_loop", ku, it * 2 + (1 + w), it)
                    down("ffn_loop", kd, it * 2 + w, w, it)
                    hidden("g", "ffn_loop", kg, it * 2 + (2 + w), it)
            hidden("u", "ffn_out", "u9", 9)
            down("ffn_out", "d8", 8, 0)
            hidden("g", "ffn_out", "g10", 10)
            hidden("u", "ffn_out", "u10", 10)
            down("ffn_out", "d9", 9, 1)
            down("ffn_out", "d10", 10, 0)
            ada(1)
            norm(2)
            pe.wait_ge(h_ready[2], 8)
            for j in range(6):
                project("cd_in", [(j, min(256, CDIN - 256 * j))], 8, CD_TILES[j], tok(H1hi, H1lo), lambda t: (j, t))
            pe.wait_ge(cn_ready, 6)
            for b_ in range(3):
                b = bank(pe, "cq", b_)
                for a_ in range(2):
                    ins = T.transpose(b[:, a_ * P:(a_ + 1) * P], Zx[:, a_, CQ0 + b_ * P:CQ0 + (b_ + 1) * P], ident[:])
                filled(ins, "cq", b_)
            for b_ in range(2):
                b = bank(pe, "ckv", b_)
                for t in range(NT):
                    src = Zx[:, t - 2, CKV0 + b_ * P:CKV0 + (b_ + 1) * P] if t >= 2 else Zt[:, t, 384 + b_ * P:384 + (b_ + 1) * P]
                    ins = T.transpose(b[:, t * P:(t + 1) * P], src, ident[:])
                filled(ins, "ckv", b_)
            pe.wait_ge(cqn_ready, 5)
            for h in range(2):
                project("uq", [(h, 384)], 3, range(2), tok(H1hi, H1lo), lambda t: (h, t))
            wh, wl = slab(pe, "ukv", 0, (2, D))
            for t in range(NT):
                for h in range(2):
                    b = bank(pe, "ukv", (t, h))
                    for k in range(2):
                        toks, cols = slice(t * P, (t + 1) * P), slice(512 * h, 512 * h + 512)
                        ins = product(pe, b[:], H1hi[:, 4 + k, toks], H1lo[:, 4 + k, toks], wh[:, k, cols], wl[:, k, cols],
                                      k == 0, k == 1)
                    if (t, h) != (3, 1):
                        filled(ins, "ukv", (t, h))
            used(ins)
            pe.wait_ge(qk_ready, 4)
            b = bank(pe, "heads", "kc")
            for t in range(NT):
                ins = T.transpose(b[:, t * P:(t + 1) * P], Zx[:, t - 2, 512:640] if t >= 2 else Zt[:, t, 0:128], ident[:])
            filled(ins, "heads", "kc")
            for i in range(2):
                b = bank(pe, "heads", ("qc", i))
                for j in range(2):
                    for a_ in range(2):
                        c0 = (2 * j + a_) * P
                        ins = T.transpose(b[:, c0:c0 + P], Zx[:, a_, (2 * i + j) * P:(2 * i + j + 1) * P], ident[:])
                filled(ins, "heads", ("qc", i))
            pe.wait_ge(kr_ready, 2)
            b = bank(pe, "heads", "kr")
            for t in range(NT):
                ins = T.transpose(b[0:32, t * P:(t + 1) * P], Zx[:, t - 2, KR0:CDIN] if t >= 2 else Zt[:, t, 640:672], ident[:])
            filled(ins, "heads", "kr")
            for h in range(8):
                b = bank(pe, "heads", ("kd", h))
                for t in range(NT):
                    await_emptied(pe, "ukv", (t, h // 4))
                    ins = T.transpose(b[0:64, t * P:(t + 1) * P], kv[:, t, h * P:h * P + 64], ident[:])
                filled(ins, "heads", ("kd", h))
            pe.wait_ge(rope_ready, 2)
            for i in range(4):
                b = bank(pe, "heads", ("qd", i))
                for j in range(2):
                    for a_ in range(2):
                        c0, h = (2 * j + a_) * P, 2 * i + j
                        ins = T.transpose(b[0:96, c0:c0 + P], qd[:, a_, 96 * h:96 * h + 96], ident[:])
                filled(ins, "heads", ("qd", i))
            for key in ["kc", "kr"] + [("qc", i) for i in range(2)] + [("kd", h) for h in range(8)] + [("qd", i) for i in range(4)]:
                await_emptied(pe, "heads", key)

            for i in range(34):
                if i < 32:
                    br, h, a_ = unit(i)
                    toks = slice(a_ * P, (a_ + 1) * P)
                    rows = slice(64 * (h // 4), 64 * (h // 4) + 64)
                    q_, k_ = (qdT[0:96, h, toks], kdT[0:96, h, :]) if br else (qcT[rows, h % 4, toks], kcT[rows, :])
                    filled(T.matmul(bank(pe, "att", ("s", i))[:], q_, k_, start=True, stop=True), "att", ("s", i))
                if 2 <= i:
                    br, h, a_ = unit(i - 2)
                    await_emptied(pe, "att", ("t", i - 2))
                    b = bank(pe, "att", ("o", i - 2))
                    for t in range(NT):
                        if br:
                            val = kv[:, t, h * P + 64:(h + 1) * P]
                        else:
                            c0 = (h // 4) * 64
                            val = Zx[:, t - 2, 640 + c0:704 + c0] if t >= 2 else Zt[:, t, 128 + c0:192 + c0]
                        ins = T.matmul(b[:, 0:64], pT[:, i % 2, t * P:(t + 1) * P], val, start=(t == 0), stop=(t == 3))
                    filled(ins, "att", ("o", i - 2))
                if 1 <= i < 33:
                    await_emptied(pe, "att", ("s", i - 1))
                    b = bank(pe, "att", ("t", i - 1))
                    for t in range(NT):
                        ins = T.transpose(b[:, t * P:(t + 1) * P], pexp[:, (i - 1) % 2, t * P:(t + 1) * P], ident[:])
                    filled(ins, "att", ("t", i - 1))
            for i in (30, 31):
                await_emptied(pe, "att", ("o", i))
            for b_ in range(4):
                b = bank(pe, "oT", b_)
                for j in range(2):
                    for a_ in range(2):
                        c0 = (2 * j + a_) * P
                        ins = T.transpose(b[:, c0:c0 + P], X[:, a_, (2 * b_ + j) * P:(2 * b_ + j + 1) * P], ident[:])
                filled(ins, "oT", b_)
            for b_ in range(4):
                await_emptied(pe, "oT", b_)
            for h in range(2):
                project("cd_out", [((h, 0), 512), ((h, 1), 512)], 4, range(2), tok(oTh, oTl), lambda t: (h, t))
            norm(3)
            for k in range(8):
                await_emptied(pe, "norm3", k)
            pe.wait_ge(experts_in, 16 * 5)
            b = bank(pe, "route", "logits")
            for t in range(2):
                for k in range(KD):
                    ins = T.matmul(b[:, t * NE:(t + 1) * NE], h2T[:, k, t * P:(t + 1) * P], router[:, k, :],
                                   start=(k == 0), stop=(k == KD - 1))
            filled(ins, "route", "logits")
            for b_ in range(4):
                b = bank(pe, "route", ("back", b_))
                for kk in range(4):
                    ins = T.transpose(b[:, kk * P:(kk + 1) * P],
                                      h2T[:, (b_ % 2) * 4 + kk, (b_ // 2) * P:(b_ // 2 + 1) * P], ident[:])
                filled(ins, "route", ("back", b_))
            pe.wait_ge(chosen_ready, 2)
            b = bank(pe, "route", "cum")
            T.matmul(b[:, 0:8], tri[:], chosen[:, 0, :], start=True, stop=True)
            T.matmul(b[:, 8:16], ones[:], chosen[:, 0, :], start=True, stop=False)
            T.matmul(b[:, 8:16], tri[:], chosen[:, 1, :], start=False, stop=True)
            T.matmul(b[:, 16:24], ones[:], chosen[:, 0, :], start=True, stop=False)
            filled(T.matmul(b[:, 16:24], ones[:], chosen[:, 1, :], start=False, stop=True), "route", "cum")
            for b_ in range(4):
                await_emptied(pe, "route", ("back", b_))

            def gather(r, stage, w, par, placed, it=0):
                pe.wait_ge(p_ready[r], placed)
                for part, src in (("xh", h2h), ("xl", h2l)):
                    for h in range(2):
                        b = bank(pe, stage, (part, w, h), it)
                        for kk in range(4):
                            k = 4 * h + kk
                            for t in range(2):
                                ins = T.matmul(b[:, kk * P:(kk + 1) * P], src[:, t, k * P:(k + 1) * P], Pm[:, par, t, :],
                                               start=(t == 0), stop=(t == 1))
                        filled(ins, stage, (part, w, h))
                b = bank(pe, stage, ("pt", w), it)
                for t in range(2):
                    ins = T.transpose(b[:, t * P:(t + 1) * P], Pm[:, par, t, :].bitcast(F32), ident[:])
                filled(ins, stage, ("pt", w))

            def features(st, kind, w, c, it):
                n_ = 512 if c < 5 else 256
                b = bank(pe, st, (kind, w, c), it)
                first = (4 * c + (2 if kind == "u" else 0)) if c < 5 else (20 if kind == "g" else 21)
                parts = 2 if c < 5 else 1
                for q in range(parts):
                    blocks = KD // parts
                    wh, wl = slab(pe, st, (w, first + q), (blocks, n_), it)
                    for k in range(blocks):
                        kk = q * blocks + k
                        ins = product(pe, b[:, 0:n_], xgh[:, kk, :], xgl[:, kk, :], wh[:, k, :], wl[:, k, :],
                                      kk == 0, kk == KD - 1)
                    used(ins)

            def turn(st, w, c, it):
                await_emptied(pe, st, ("u", w, c), it)
                b = bank(pe, st, ("t", w, c), it)
                for j in range(4 if c < 5 else 2):
                    ins = T.transpose(b[:, j * P:(j + 1) * P], ame[:, c % 2, j * P:(j + 1) * P], ident[:])
                filled(ins, st, ("t", w, c))

            def down_e(st, w, it):
                out_banks = [bank(pe, st, ("d", w, h), it) for h in range(2)]
                for j in range(11):
                    await_emptied(pe, st, ("t", w, (2 * j + 1) // 4), it)
                    wh, wl = slab(pe, st, (w, 22 + j), (2, D), it)
                    for h in range(2):
                        for k in range(2):
                            kk, cols = 2 * j + k, slice(512 * h, 512 * h + 512)
                            ins = product(pe, out_banks[h][:], aTh[:, kk, :], aTl[:, kk, :], wh[:, k, cols], wl[:, k, cols],
                                          kk == 0, kk == 21)
                        if j == 10 and h == 0:
                            filled(ins, st, ("d", w, 0))
                    used(ins)

            def scatter(st, w, it):
                for h in range(2):
                    await_emptied(pe, st, ("d", w, h), it)
                for o in range(4):
                    t, h = o // 2, o % 2
                    b = bank(pe, st, ("y", w, o), it)
                    T.matmul(b[:], PT[:, w, t, :], yeh[:, h, :], start=True, stop=False)
                    filled(T.matmul(b[:], PT[:, w, t, :], yel[:, h, :], start=False, stop=True), st, ("y", w, o))

            def expert(st, w, it):
                for key in (("xl", 1 - w, 1), ("pt", 1 - w)):
                    if st == "over" or w == 1:
                        await_emptied(pe, st, key, it)
                for c in range(6):
                    features(st, "g", w, c, it)
                    features(st, "u", w, c, it)
                    if w == 1 and c == 0:
                        scatter(st, 0, it)
                    if c:
                        turn(st, w, c - 1, it)
                if st == "moe":
                    gather(0, st, w, 1 - w, it * 4 + (2 * w + 4), it)
                turn(st, w, 5, it)
                down_e(st, w, it)
            gather(0, "first", 1, 0, 2)
            for key in (("xl", 1, 1), ("pt", 1)):
                await_emptied(pe, "first", key)
            with pe.Fori(0, NE // 2) as it:
                expert("moe", 0, it)
                expert("moe", 1, it)
                scatter("moe", 1, it)
                for key in (("xl", 1, 1), ("pt", 1)):
                    await_emptied(pe, "moe", key, it)
            pe.wait_ge(routed, 1)
            with pe.Fori(0, OVER) as j:
                more = pe.value_load(over_i[0:1, 0, bass.ds(j, 1)], min_val=0, max_val=NE)
                with pe.If(more > 0):
                    gather(1, "over", 1, 0, j * 2 + 2, j)
                    expert("over", 0, j)
                    scatter("over", 0, j)


_INS = ["x", "c", "ctx", "c_ctx", "ada_w", "ada_b", "ab_w_in", "a_v_gain", "a_w_s", "a_b_s", "b_w_pool", "b_scale",
        "ab_w_out", "ffn_w_gate", "ffn_w_up", "ffn_w_down", "cd_w_in", "c_q_gain", "c_k_gain", "d_cq_gain",
        "d_ckv_gain", "d_w_uq", "d_w_ukv", "cd_w_out", "moe_router", "moe_w_gate", "moe_w_up", "moe_w_down", "final_gain"]


def kernel(**inputs):
    import concourse.bacc as bacc
    from concourse.bass_utils import run_bass_kernel_spmd

    nc = bacc.Bacc("TRN2", target_bir_lowering=False, num_devices=1)
    arrays, args = {}, {}
    given = {name: np.ascontiguousarray(inputs[name]) for name in _INS}
    given.update(shape_tables())
    for name, value in given.items():
        arrays[f"in_{name}_dram"] = value
        args[name] = nc.dram_tensor(f"in_{name}_dram", value.shape, mybir.dt.from_np(value.dtype), kind="ExternalInput").ap()
    out = nc.dram_tensor("out_0_dram", (1, SEQ, D), F32, kind="ExternalOutput").ap()
    build(nc, args, out)
    r = run_bass_kernel_spmd(nc, [arrays], core_ids=[0])
    return r.results[0]["out_0_dram"]
```

```python
from contextlib import ExitStack

import numpy as np

import concourse.bass as bass
from concourse import mybir

F32 = mybir.dt.float32
F32R = mybir.dt.float32r
I32 = mybir.dt.int32
U32 = mybir.dt.uint32
ALU = mybir.AluOpType
ACT = mybir.ActivationFunctionType
AX = mybir.AxisListType.X

P = 128
D = 1024
KD = D // P
SEQ = 256
NT = 4
EPS = 1e-6
GRID_W = 64
ROPE_THETA = 10000.0
AW = 512
POOL_WINDOWS = (2, 4, 8, 16)
FF = 2816
NE = 8
SLOTS = 128
ROUNDS = SEQ // SLOTS
CAP = SLOTS
OVER = 2 * SEQ // (SLOTS + 1)
GATE_BLOCKS = (4, 5, 10, 11)
EARLY, LATE = range(4), range(4, 12)
KIND = {0: 0, 1: 1, 3: 2, 4: 3}
LOOP_KEYS = (("uA", "dA", "gA"), ("uB", "dB", "gB"))
OUT_KEYS = (("u9", "d8", "g10"), ("u10", "d9", "d10"))
CD_TILES = [range(4) if j in (2, 4, 5) else range(2, 4) for j in range(6)]
ZT0 = {2: 0, 4: 256, 5: 512}
CQ0, CKV0, KR0, CDIN = 768, 1152, 1408, 1440
RAW, SPL = 6, 3
SLAB = 2048
FFI = FF // 256


FIRST_SLABS = [("ada0", (cb, h)) for cb in range(4) for h in range(2)]
MIX_SLABS = []
for j_ in range(6):
    MIX_SLABS += [("ab_in", j_)] + [("ada0", (4 + j_, h)) for h in range(2)]
MIX_SLABS += [("ada0", (cb, h)) for cb in (10, 11) for h in range(2)]
MIX_SLABS += [("ada1", (cb, h)) for cb in (0, 1) for h in range(2)]
MIX_SLABS += [("ab_out", (h, q)) for h in range(2) for q in range(2)]
MIX_SLABS += [("ada1", (cb, h)) for cb in (2, 3) for h in range(2)]


def slab_order():
    ffn = [("ffn_in", 1, ["g0", "u0", "g1"]),
           ("ffn_loop", 4, ["uA", "dA", "gA", "uB", "dB", "gB"]),
           ("ffn_out", 1, ["u9", "d8", "g10", "u10", "d9", "d10"])]
    expert = [(w, s) for w in range(2) for s in range(33)]
    return ([(stage, 1, [key]) for stage, key in FIRST_SLABS + MIX_SLABS] + ffn +
            [("cd_in", 1, list(range(6))), ("uq", 1, [0, 1]), ("ukv", 1, [0]),
             ("late", 1, [(cb, h) for cb in LATE for h in range(2)]),
             ("cd_out", 1, [(h, q) for h in range(2) for q in range(2)])] +
            [("moe", NE // 2, expert), ("over", OVER, [(0, s) for s in range(33)])])


def bank_order():
    out = []

    out.append(("start", 1, [("cT", 0)]))
    for layer, blocks in ((0, range(12)), (1, EARLY)):
        for cb in blocks:
            out.append((f"ada{layer}", 1, [(("m", cb), 5 + cb % 2, (cb, 1))]))
            out.append((f"ada{layer}", 1, [(("bc", cb, who), 7) for who in range(2)] if cb in GATE_BLOCKS else [(("col", cb), 7)]))
    out.append(("norm0", 1, [(k, k % 5) for k in range(8)]))
    out.append(("wsT", 1, [("wsT", 4)]))
    out.append(("ab_in", 1, [((j, t), (4 * j + t) % 5) + ((j,) if t == 3 else ()) for j in range(6) for t in range(NT)]))
    out.append(("ab_s", 1, [(t, t) for t in range(NT)]))
    for g in (0, 1, 2, 3, 4):
        out.append(("ab_pool", 1, [(g, g)] if g < 4 else []))
        out.append(("ab_yb", 1, [(g - 1, (3 + g) % 5)] if g >= 1 else []))
    out.append(("ab_ya", 1, [(g, (3 + g) % 5) for g in range(4)]))
    out.append(("ab_out", 1, [((h, t), (4 * h + t) % 5) + (((h, 1),) if t == 3 else ()) for h in range(2) for t in range(NT)]))
    out.append(("norm1", 1, [(k, k % 5) for k in range(8)]))

    out.append(("ffn", FFI, [((kind, b), n + b) + ((kind,) if b else ()) for kind, n in (("g", 0), ("u", 2)) for b in range(2)] +
                [(("d", o), 4 + o % 4) + (("d",) if o == 7 else ()) for o in range(8)]))
    out.append(("norm2", 1, [(k, k) for k in range(8)]))
    uses = [(j, t) for j in range(6) for t in range(NT) if t >= 2 or j in (2, 4, 5)]
    out.append(("cd_in", 1, [(u, n % 8) + ((u[0],) if u[1] == 3 else ()) for n, u in enumerate(uses)]))
    out.append(("cq", 1, [(b, b) for b in range(3)]))
    out.append(("ckv", 1, [(b, 4 + b) for b in range(2)]))
    out.append(("uq", 1, [((h, a), 2 * h + a) + ((h,) if a else ()) for h in range(2) for a in range(2)]))
    out.append(("ukv", 1, [((t, h), (4 + 2 * t + h) % 8) + ((0,) if (t, h) == (3, 1) else ()) for t in range(NT) for h in range(2)]))
    out.append(("heads", 1, [("kc", 0), (("qc", 0), 1), (("qc", 1), 2), ("kr", 3)] +
                [(("kd", h), 4 + h % 4) for h in range(8)] + [(("qd", h), h % 4) for h in range(4)]))
    att = []
    for i in range(34):
        if i < 32:
            att.append((("s", i), i % 2))
        if 2 <= i:
            att.append((("o", i - 2), 5 + i % 2))
        if 1 <= i < 33:
            att.append((("t", i - 1), 3 + (i - 1) % 2))
    out.append(("att", 1, att))
    out.append(("late", 1, [(("m", cb), 7, (cb, 1)) for cb in LATE] +
                [((("bc", cb, 0) if cb in GATE_BLOCKS else ("col", cb)), 2) for cb in LATE]))
    out.append(("oT", 1, [(b, b) for b in range(4)]))
    out.append(("cd_out", 1, [((h, a), 4 + 2 * h + a) + (((h, 1),) if a else ()) for h in range(2) for a in range(2)]))
    out.append(("norm3", 1, [(k, k) for k in range(8)]))
    out.append(("route", 1, [("logits", 0), ("cum", 1), (("back", 0), 2), (("back", 1), 3), (("back", 2), 4),
                             (("back", 3), 5)]))

    def gather(w):
        return [(("xh", w, 0), 5), (("xh", w, 1), 4), (("xl", w, 0), 5), (("xl", w, 1), 4), (("pt", w), 5)]

    def scatter(w):
        return [(("y", w, o), 5 - o % 2) for o in range(4)]

    def expert(w, middle, between):
        body = []
        for c in range(6):
            body += [(("g", w, c), c % 2, (w, 4 * c + 1 if c < 5 else 20)), (("u", w, c), 2 + c % 2, (w, 4 * c + 3 if c < 5 else 21))]
            if c == 0:
                body += middle
            if c >= 1:
                body.append((("t", w, c - 1), 4 + (c - 1) % 2))
        return body + between + [(("t", w, 5), 4), (("d", w, 0), 6), (("d", w, 1), 7, (w, 32))]
    out.append(("first", 1, gather(1)))
    out.append(("moe", NE // 2, expert(0, [], gather(0)) + expert(1, scatter(0), gather(1)) + scatter(1)))
    out.append(("over", OVER, gather(1) + expert(0, [], []) + scatter(0)))
    return out


def shape_tables():
    f = np.float32
    t = {}
    sel = np.zeros((5, 2, P), f)
    for who in range(2):
        sel[[who, who + 2, 4], who, :] = 1
    t["k_sel"] = sel
    t["k_ident"] = np.eye(P, dtype=f)
    t["k_ones"] = np.ones((P, P), f)
    t["k_tri"] = np.triu(np.ones((P, P), f))
    t["k_slot"] = np.tile(np.arange(ROUNDS * SLOTS, dtype=f), (P, 1))
    t["k_expert"] = np.tile(np.arange(NE, dtype=f), (P, 1))
    band = np.zeros((SEQ, 4, SEQ), f)
    pos = np.arange(SEQ)
    for g, w in enumerate(POOL_WINDOWS):
        lo = np.clip(pos - w // 2, 0, SEQ)
        hi = np.clip(pos - w // 2 + w, 0, SEQ)
        inside = (pos[:, None] >= lo[None]) & (pos[:, None] < hi[None])
        band[:, g] = np.where(inside, f(1) / (hi - lo).astype(f), f(0)) - np.eye(SEQ, dtype=f)
    t["k_band"] = np.stack([band[a * P:(a + 1) * P, :, a * 112:a * 112 + 144] for a in range(2)], 2).copy()
    rows = np.repeat(np.arange(SEQ // GRID_W), GRID_W).astype(f)
    cols = np.tile(np.arange(GRID_W), SEQ // GRID_W).astype(f)
    for name, dim in (("k_ropec", 64), ("k_roped", 32)):
        axis = dim // 2
        inv = (f(ROPE_THETA) ** (-np.arange(0, axis, 2, dtype=f) / f(axis))).astype(f)
        ang = np.concatenate([rows[:, None] * inv, cols[:, None] * inv], -1)
        c, s = np.cos(ang), np.sin(ang)
        both = np.stack([np.concatenate([c, c], -1), np.concatenate([-s, s], -1)], 1)
        t[name] = both.reshape(2, P, 2, dim).transpose(1, 0, 2, 3).astype(f).copy()
    return t


class Count:

    def __init__(self, eng, sem):
        self.eng, self.sem, self.n, self.it, self.per, self.at = eng, sem, 0, None, 0, 0

    def mark(self, ins):
        ins.then_inc(self.sem, 1)
        self.n += 1

    def wait(self):
        self.eng.wait_ge(self.sem, self.n if self.it is None else self.it * self.per + self.n)

    def enter(self, it, per):
        self.it, self.per, self.at = it, per, self.n

    def leave(self, times):
        assert self.n - self.at == self.per, (self.n - self.at, self.per)
        self.n, self.it = self.at + times * self.per, None


def build(nc, a, out):
    slabs, n, landed = {}, 0, [0] * RAW
    for stage, times, keys in slab_order():
        depth = RAW if times == 1 or len(keys) % RAW == 0 else SPL
        assert times == 1 or len(keys) % depth == 0
        slots = [(n + i) % depth for i in range(len(keys))]
        for i, key in enumerate(keys):
            slabs[stage, key] = (n + i, len(keys), slots[i], landed[slots[i]] + slots[:i].count(slots[i]),
                                 slots.count(slots[i]), depth)
        landed = [landed[b] + times * slots.count(b) for b in range(RAW)]
        n += times * len(keys)
    banks, at, signals = {}, [0] * 8, [0] * 8
    for stage, times, uses in bank_order():
        per = [sum(u[1] == b for u in uses) for b in range(8)]
        per_signal = [sum(u[1] == b and len(u) == 2 for u in uses) for b in range(8)]
        use, signal = list(at), list(signals)
        for key, b, *closing in uses:
            assert (stage, key) not in banks
            banks[stage, key] = (b, use[b], per[b], signal[b], per_signal[b], closing[0] if closing else None)
            use[b] += 1
            signal[b] += not closing
        at = [at[b] + times * per[b] for b in range(8)]
        signals = [signals[b] + times * per_signal[b] for b in range(8)]

    with ExitStack() as ctx:
        def sem(name):
            return ctx.enter_context(nc.semaphore(name))

        def sb(name, shape, dt=F32, into=None):
            return (into or ctx).enter_context(nc.sbuf_tensor(name, shape, dt))

        raw = [sb(f"raw{i}", [P, SLAB]) for i in range(RAW)]
        hi = [sb(f"hi{i}", [P, SLAB], F32R) for i in range(SPL)]
        lo = [sb(f"lo{i}", [P, SLAB], F32R) for i in range(SPL)]
        X = sb("X", [P, NT, D])
        ident = sb("ident", [P, P])
        sel = sb("sel", [5, 2, P])
        crows = sb("crows", [29, P])
        C4 = sb("C4", [P, KD, 4], F32R)
        cs = sb("cs", [P, 16])
        mrow = sb("mrow", [P, 2, 512])
        modcol = [sb(f"modcol{i}", [P, 4, KD, 2]) for i in range(2)]
        ropec = sb("ropec", [P, 2, 2, 64])
        roped = sb("roped", [P, 2, 2, 32])
        q_gain = sb("q_gain", [P, 64])
        k_gain = sb("k_gain", [P, 64])
        pcols = sb("pcols", [P, 13])
        bs_col, bscale_col, cq_gain, ckv_gain = pcols[:, 0:4], pcols[:, 4:8], pcols[:, 8:11], pcols[:, 11:13]
        ssq = sb("ssq", [P, NT, 12])
        rstd = sb("rstd", [P, NT, 12])
        root = sb("root", [P, NT, 12])
        rowmax = sb("rowmax", [P, 2, 32])
        rowsum = sb("rowsum", [P, 2, 32])
        ps = [ctx.enter_context(nc.psum_tensor(f"bank{i}", [P, 512], F32)) for i in range(8)]

        zone = ExitStack()
        gates = [sb(f"gate_rows{w}", [P, 2, D], into=zone) for w in range(2)]
        Hhi = sb("Hhi", [P, KD, 512], F32R, zone)
        Hlo = sb("Hlo", [P, KD, 512], F32R, zone)
        free0 = ExitStack()
        u = sb("u", [P, NT, AW], into=free0)
        v = sb("v", [P, NT, AW], into=free0)
        zp = sb("zp", [P, NT, AW], into=free0)
        vgain = sb("vgain", [P, AW], into=free0)
        band = sb("band", [P, 4, 2, 144], into=free0)
        wsT = sb("wsT", [P, 4, P], into=free0)
        wpool = sb("wpool", [P, 4, P], into=free0)
        vsq = zp[:, 2, :]
        htmpA = zp[:, 0:2, :]
        ws = zp[:, 3, :].rearrange("p (g q) -> p g q", g=4)
        pooledT = v[:, 0:2, :]
        ybtmp = v[:, 2:4, :]
        free0.close()
        free1 = ExitStack()
        acth = sb("acth", [P, 2, 2, 512], F32R, free1)
        actl = sb("actl", [P, 2, 2, 512], F32R, free1)
        yacc = sb("yacc", [P, NT, D], into=free1)
        sg = mrow
        am = sb("am", [P, 2, 512], into=free1)
        free1.close()
        zone.close()
        zone1 = ExitStack()
        gates1 = sb("gates1", [P, 2, D], into=zone1)
        H1hi = sb("H1hi", [P, KD, 512], F32R, zone1)
        H1lo = sb("H1lo", [P, KD, 512], F32R, zone1)
        Zx = sb("Zx", [P, 2, CDIN], into=zone1)
        Zt = sb("Zt", [P, 2, 672], into=zone1)
        qd = sb("qd", [P, 2, 768], into=zone1)
        kv = sb("kv", [P, NT, D], into=zone1)
        pexp = sb("pexp", [P, 2, 512], into=zone1)
        pT = mrow
        zone1.close()
        zone2 = ExitStack()
        sb("gates1_again", [P, 2, D], into=zone2)
        kdT = sb("kdT", [P, 8, 512], into=zone2)
        qdT = sb("qdT", [P, 8, 256], into=zone2)
        kcT = sb("kcT", [P, 512], into=zone2)
        qcT = sb("qcT", [P, 4, 256], into=zone2)
        late_row = sb("late_row", [P, 512], into=zone2)
        zone2.close()
        zone3 = ExitStack()
        sb("gates1_third", [P, 2, D], into=zone3)
        oTh = sb("oTh", [P, KD, 256], F32R, zone3)
        oTl = sb("oTl", [P, KD, 256], F32R, zone3)
        zone3.close()
        zone4 = ExitStack()
        sb("gates1_last", [P, 2, D], into=zone4)
        h2h = sb("h2h", [P, 2, D], F32R, zone4)
        h2l = sb("h2l", [P, 2, D], F32R, zone4)
        xgh = sb("xgh", [P, KD, P], F32R, zone4)
        xgl = sb("xgl", [P, KD, P], F32R, zone4)
        yeh = sb("yeh", [P, 2, 512], F32R, zone4)
        yel = sb("yel", [P, 2, 512], F32R, zone4)
        Pm = sb("Pm", [P, 2, 2, P], F32R, zone4)
        PT = sb("PT", [P, 2, 2, P], F32R, zone4)
        sge = sb("sge", [P, 2, 512], into=zone4)
        ame = sb("ame", [P, 2, 512], into=zone4)
        logits = sb("logits", [P, 2, NE], into=zone4)
        top = sb("top", [P, 2, 8], into=zone4)
        topi = sb("topi", [P, 2, 8], U32, zone4)
        topf = sb("topf", [P, 2, 8], into=zone4)
        wts = sb("wts", [P, 2, 4], into=zone4)
        pick = sb("pick", [P, 2, 2, NE], into=zone4)
        chosen = sb("chosen", [P, 2, NE], into=zone4)
        posn = sb("posn", [P, 2, NE + 1], into=zone4)
        gate_e = sb("gate_e", [P, 2, NE], into=zone4)
        over = sb("over", [P, 3, NE], into=zone4)
        over_i = sb("over_i", [P, 2, NE], I32, zone4)
        fgain = sb("fgain", [P, D], into=zone4)
        ones = sb("ones", [P, P], into=zone4)
        tri = sb("tri", [P, P], into=zone4)
        slot_row = sb("slot_row", [P, ROUNDS * SLOTS], into=zone4)
        expert_row = sb("expert_row", [P, NE], into=zone4)
        router = sb("router", [P, KD, NE], into=zone4)
        zone5 = ExitStack()
        h2T = sb("h2T", [P, KD, 256], into=zone5)
        xnM = sb("xnM", [P, 2, D], into=zone5)
        zone5.close()
        aTh = sb("aTh", [P, 22, P], F32R, zone4)
        aTl = sb("aTl", [P, 22, P], F32R, zone4)
        zone4.close()
        yM = X[:, 0:2, :]

        raw_in = [sem(f"raw_in{i}") for i in range(RAW)]
        hi_ready, slab_used = sem("hi_ready"), sem("slab_used")
        lo_dve = [sem(f"lo_dve{i}") for i in range(SPL)]
        lo_pool = [sem(f"lo_pool{i}") for i in range(SPL)]
        bank_full = [sem(f"bank_full{i}") for i in range(8)]
        bank_emptied = [sem(f"bank_emptied{i}") for i in range(8)]
        c_in, sel_in, x_in, ident_in, ab_consts = sem("c_in"), sem("sel_in"), sem("x_in"), sem("ident_in"), sem("ab_consts")
        ssq_clear, cqn_ready, cn_ready, kr_ready, logit_diff = (sem(n_) for n_ in (
            "ssq_clear", "cqn_ready", "cn_ready", "kr_ready", "logit_diff"))
        experts_in = sem("experts_consts_in")
        l1_in, fgain_in, bias_in = sem("layer1_consts_in"), sem("fgain_in"), [sem(f"bias_in{i}") for i in range(2)]
        first_bias_in = sem("first_bias_in")
        silu_c, c_hi, c_lo = sem("silu_c"), sem("c_hi"), sem("c_lo")
        dve_chain, act_chain = sem("dve_chain"), sem("act_chain")
        sumsq = [sem(f"sumsq{i}") for i in range(7)]
        meansq = [sem(f"meansq{i}") for i in range(7)]
        rooted = [sem(f"rooted{i}") for i in range(7)]
        xn_ready = [sem(f"xn_ready{i}") for i in range(4)]
        h_ready = [sem(f"h_ready{i}") for i in range(4)]
        x_ready = [sem(f"x_ready{i}") for i in range(4)]
        v_ready, ya_hi, y_ready = sem("v_ready"), sem("ya_hi"), sem("y_ready")
        ff_ready, qk_ready, rope_ready = sem("ff_ready"), sem("qk_ready"), sem("rope_ready")
        negmax, exped, o_ready, oT_hi = sem("negmax"), sem("exped"), sem("o_ready"), sem("oT_hi")
        h2_hi, routed = sem("h2_hi"), sem("routed")
        chosen_ready, gexp = sem("chosen_ready"), sem("gate_exp")
        p_ready = [sem(f"p_ready{r}") for r in range(ROUNDS)]
        hi_out = [sem(f"hi_out{r}") for r in range(ROUNDS)]
        summed, y_done, fin_ready, stored = sem("summed"), sem("y_done"), sem("fin_ready"), sem("stored")

        def view(t, shape):
            k, f = shape
            return t[:, 0:k * f].rearrange("p (k f) -> p k f", k=k)

        def load(sp, stage, key, src, it=0):
            n0, per, slot, _, _, depth = slabs[stage, key]
            if n0 >= depth:
                before = (n0 - depth) // SPL + 1 + it * (per // SPL)
                sp.wait_ge(lo_dve[n0 % SPL], before)
                sp.wait_ge(lo_pool[n0 % SPL], before)
                if not isinstance(it, int):
                    sp.wait_ge(hi_ready, n0 - depth + 1)
            _, k, f = src.shape
            sp.dma_start(view(raw[slot], (k, f)), src).then_inc(raw_in[slot], 16)

        def split_hi(act, stage, key, size=SLAB, it=0):
            n0, per, slot, use, uses, _ = slabs[stage, key]
            act.wait_ge(raw_in[slot], 16 * (use + 1) + it * (16 * uses))
            if n0 >= SPL:
                act.wait_ge(slab_used, n0 - SPL + 1 + it * per)
            nc.scalar.activation(hi[n0 % SPL][:, 0:size], raw[slot][:, 0:size], ACT.Copy).then_inc(hi_ready, 1)

        def split_lo(eng, stage, key, size=SLAB, it=0):
            n0, per, slot, _, _, _ = slabs[stage, key]
            at = size * 5 // 8
            cols, ready = (slice(at, size), lo_pool) if eng is nc.gpsimd else (slice(0, at), lo_dve)
            eng.wait_ge(hi_ready, n0 + 1 + it * per)
            eng.tensor_tensor(lo[n0 % SPL][:, cols], raw[slot][:, cols], hi[n0 % SPL][:, cols].bitcast(F32),
                              ALU.subtract).then_inc(ready[n0 % SPL], 1)

        def slab(pe, stage, key, shape, it=0):
            n0, per = slabs[stage, key][:2]
            there = n0 // SPL + 1 + it * (per // SPL)
            pe.wait_ge(lo_dve[n0 % SPL], there)
            pe.wait_ge(lo_pool[n0 % SPL], there)
            return view(hi[n0 % SPL], shape), view(lo[n0 % SPL], shape)

        def bank(pe, stage, key, it=0):
            b, r, per = banks[stage, key][:3]
            if r:
                pe.wait_ge(bank_emptied[b], r + it * per)
            return ps[b]

        def filled(ins, stage, key):
            assert banks[stage, key][5] is None
            ins.then_inc(bank_full[banks[stage, key][0]], 1)

        def full(eng, stage, key, it=0):
            b, _, _, r, per, closing = banks[stage, key]
            if closing is None:
                eng.wait_ge(bank_full[b], r + 1 + it * per)
            elif stage == "ffn":
                eng.wait_ge(slab_used, ffn_slab(closing, it) + 1)
            else:
                n0, per = slabs[stage, closing][:2]
                eng.wait_ge(slab_used, n0 + 1 + it * per)
            return ps[b]

        def ffn_slab(kind, i):
            n = slabs["ffn_in", "g0"][0]
            if isinstance(i, int):
                return n + {"g": max(3 * i - 1, 0), "u": max(3 * i, 1), "d": min(3 * i + 4, 3 * FFI - 1)}[kind]
            return i * 3 + (n + {"g": -1, "u": 0, "d": 4}[kind])

        def emptied(ins, stage, key):
            ins.then_inc(bank_emptied[banks[stage, key][0]], 1)

        def await_emptied(eng, stage, key, it=0):
            b, r, per = banks[stage, key][:3]
            eng.wait_ge(bank_emptied[b], r + 1 + it * per)

        def product(pe, dst, lh, ll, rh, rl, first, last):
            nc.tensor.matmul(dst, lh, rh, start=first, stop=False, skip_group_check=True)
            nc.tensor.matmul(dst, lh, rl, start=False, stop=False, skip_group_check=True)
            return nc.tensor.matmul(dst, ll, rh, start=False, stop=last, skip_group_check=True)

        NORM_TILES = [range(4), range(4), range(4), range(2, 4)]

        def norm_scratch(i):
            if i == 0:
                return ([u[:, 0:2, :], u[:, 2:4, :], v[:, 0:2, :], v[:, 2:4, :]], htmpA)
            if i == 1:
                return ([yacc[:, t, :] for t in range(4)], sg)
            if i == 2:
                return ([kv[:, t, :] for t in range(4)], pexp)
            return ([None, None, xnM[:, 0, :], xnM[:, 1, :]], sge)

        def xt(i, t):
            return X[:, t, :].rearrange("p (a b) -> p a b", a=2) if i == 0 else X[:, t, :]

        def H_of(i):
            return (H1hi, H1lo) if i == 2 else (Hhi, Hlo)

        COMPRESSED = [("cq", b_, 256, b_) for b_ in range(3)] + [("ckv", b_, 512, 4 + b_) for b_ in range(2)]

        def slab_size(stage, key):
            return {"uq": 3 * 384, "cd_in": 8 * min(256, CDIN - 256 * key) if stage == "cd_in" else 0}.get(stage, SLAB)

        def ada_stage(layer, cb):
            return "late" if layer == 1 and cb in LATE else f"ada{layer}"

        def mod_rows(st, cb):
            if st == "late":
                return late_row[0:5, :]
            return (zp if st == "ada0" and cb in (2, 3) else mrow)[0:5, cb % 2, :]

        def spread(cb, who=0):
            return ("bc", cb, who) if cb in GATE_BLOCKS else ("col", cb)

        def before(layer, cb):
            if layer == 0:
                last = {4: 0, 5: 1}.get(cb, cb - 2)
                return ("ada0", spread(last, 1)) if cb >= 4 else None
            return ("ada1", spread(cb - 2)) if cb >= 2 else ("ada0", spread(10 + cb, 1))

        def late_block(i):
            return LATE[i // 4]

        LATE_SLABS = [("late", (cb, h)) for cb in LATE for h in range(2)] + [("cd_out", (h, q)) for h in range(2) for q in range(2)]

        def unit(i):
            return i // 16, i // 2 % 8, i % 2

        def att_scale(i):
            return (64 if i < 16 else 96) ** -0.5

        def xn_block(i, t, k):
            x = norm_scratch(i)[0][t]
            return x[:, k // 4, (k % 4) * P:(k % 4 + 1) * P] if i == 0 else x[:, k * P:(k + 1) * P]

        def xn_all(i, t):
            return norm_scratch(i)[0][t]

        def columns(w, k, f0, f1):
            return w.rearrange("(k p) f -> p k f", p=P)[:, k, f0:f1]

        def expert_slabs(w):
            s = []
            for c in range(5):
                for kind in "gu":
                    for q in range(2):
                        s.append((kind, c, slice(4 * q, 4 * q + 4), slice(512 * c, 512 * c + 512)))
            s += [(kind, 5, slice(0, 8), slice(2560, 2816)) for kind in "gu"]
            s += [("d", j, slice(2 * j, 2 * j + 2), slice(0, D)) for j in range(11)]
            return s
        ES = expert_slabs(0)

        block = ctx.enter_context(nc.Block())

        @block.sync
        def _(sp):
            def ada(layer, key):
                cb, h = key
                load(sp, ada_stage(layer, cb), key, columns(a["ada_w"][layer], slice(4 * h, 4 * h + 4), 512 * cb, 512 * cb + 512))

            sp.dma_start(crows[0:8, :], a["c"].rearrange("b (k p) -> (b k) p", p=P)).then_inc(c_in, 16)
            sp.dma_start(crows[8:16, :], a["c_ctx"].rearrange("(k p) -> k p", p=P)).then_inc(c_in, 16)
            sp.dma_start(crows[16:20, :], a["a_b_s"][0]).then_inc(c_in, 16)
            sp.dma_start(crows[20:24, :], a["b_scale"][0].rearrange("(k p) -> k p", p=P)).then_inc(c_in, 16)
            sp.dma_start(crows[24:27, :], a["d_cq_gain"][0].rearrange("(k p) -> k p", p=P)).then_inc(c_in, 16)
            sp.dma_start(crows[27:29, :], a["d_ckv_gain"][0].rearrange("(k p) -> k p", p=P)).then_inc(c_in, 16)
            sp.dma_start(ident[:], a["k_ident"]).then_inc(ident_in, 16)
            for cb in range(4):
                sp.dma_start(mod_rows("ada0", cb)[4:5], a["ada_b"][0:1, 512 * cb:512 * cb + 512]).then_inc(first_bias_in, 16)
            for stage, key in FIRST_SLABS + MIX_SLABS:
                if stage == "ab_in":
                    load(sp, stage, key, columns(a["ab_w_in"][0], slice(0, 8), 256 * key, 256 * key + 256))
                elif stage == "ab_out":
                    h, q = key
                    load(sp, stage, key, columns(a["ab_w_out"][0], slice(4 * q, 4 * q + 4), 512 * h, 512 * h + 512))
                else:
                    ada(int(stage == "ada1"), key)
            wg, wu, wd = (a[n][0].rearrange("(k p) f -> p k f", p=P) for n in ("ffn_w_gate", "ffn_w_up", "ffn_w_down"))

            def gate(stage, key, w, i, it=0):
                load(sp, stage, key, w[:, :, bass.ds(i * 256, 256)], it)

            def down(stage, key, i, it=0):
                load(sp, stage, key, wd[:, bass.ds(i * 2, 2), :], it)
            gate("ffn_in", "g0", wg, 0)
            gate("ffn_in", "u0", wu, 0)
            gate("ffn_in", "g1", wg, 1)
            with sp.Fori(0, 4) as it:
                for w, name in enumerate("AB"):
                    gate("ffn_loop", "u" + name, wu, it * 2 + (w + 1), it)
                    down("ffn_loop", "d" + name, it * 2 + w, it)
                    gate("ffn_loop", "g" + name, wg, it * 2 + (w + 2), it)
            gate("ffn_out", "u9", wu, 9)
            down("ffn_out", "d8", 8)
            gate("ffn_out", "g10", wg, 10)
            gate("ffn_out", "u10", wu, 10)
            down("ffn_out", "d9", 9)
            down("ffn_out", "d10", 10)
            for j in range(6):
                load(sp, "cd_in", j, columns(a["cd_w_in"][0], slice(0, 8), 256 * j, min(256 * j + 256, CDIN)))
            for h in range(2):
                load(sp, "uq", h, columns(a["d_w_uq"][0], slice(0, 3), 384 * h, 384 * h + 384))
            load(sp, "ukv", 0, columns(a["d_w_ukv"][0], slice(0, 2), 0, D))
            for cb in LATE:
                for h in range(2):
                    ada(1, (cb, h))
            for h in range(2):
                for q in range(2):
                    load(sp, "cd_out", (h, q), columns(a["cd_w_out"][0], slice(4 * q, 4 * q + 4), 512 * h, 512 * h + 512))
            mw = {k: a[n][0].rearrange("e (k p) f -> e p k f", p=P)
                  for k, n in (("g", "moe_w_gate"), ("u", "moe_w_up"), ("d", "moe_w_down"))}

            def expert(stage, w, e, it):
                for s, (kind, _, ks, fs) in enumerate(ES):
                    load(sp, stage, (w, s), mw[kind][bass.ds(e, 1), :, ks, fs].rearrange("e p k f -> p (e k) f"), it)
            with sp.Fori(0, NE // 2) as it:
                for w in range(2):
                    expert("moe", w, it * 2 + w, it)
            sp.wait_ge(routed, 1)
            with sp.Fori(0, OVER) as j:
                more = sp.value_load(over_i[0:1, 0, bass.ds(j, 1)], min_val=0, max_val=NE)
                with sp.If(more > 0):
                    expert("over", 0, sp.value_load(over_i[0:1, 1, bass.ds(j, 1)], min_val=0, max_val=NE - 1), j)
            for t in range(2):
                sp.wait_ge(fin_ready, t + 1)
                sp.dma_start(out[0, t * P:(t + 1) * P, :], yM[:, t, :]).then_inc(stored, 16)
            sp.wait_ge(stored, 32)

        @block.gpsimd
        def _(pool):
            def bias(layer, cb):
                if cb == LATE[0] and layer == 1:
                    full(pool, "ukv", (3, 1))
                elif ada_stage(layer, cb) == "late":
                    full(pool, "late", spread(cb - 1))
                elif before(layer, cb):
                    full(pool, *before(layer, cb))
                pool.dma_start(mod_rows(ada_stage(layer, cb), cb)[4:5], a["ada_b"][layer:layer + 1, 512 * cb:512 * cb + 512]
                               ).then_inc(bias_in[cb % 2], 16)

            for stage, key in FIRST_SLABS + MIX_SLABS:
                split_lo(nc.gpsimd, stage, key)
                if stage in ("ada0", "ada1") and key[1] == 1 and (stage, key) not in FIRST_SLABS:
                    bias(int(stage == "ada1"), key[0])
            for key in ("g0", "u0", "g1"):
                split_lo(nc.gpsimd, "ffn_in", key)
            with pool.Fori(0, 4) as it:
                for key in ("uA", "dA", "gA", "uB", "dB", "gB"):
                    split_lo(nc.gpsimd, "ffn_loop", key, it=it)
            for key in ("u9", "d8", "g10", "u10", "d9", "d10"):
                split_lo(nc.gpsimd, "ffn_out", key)
            for j in range(6):
                split_lo(nc.gpsimd, "cd_in", j, 8 * min(256, CDIN - 256 * j))
            for h in range(2):
                split_lo(nc.gpsimd, "uq", h, 3 * 384)
            split_lo(nc.gpsimd, "ukv", 0)
            for cb in LATE:
                for h in range(2):
                    split_lo(nc.gpsimd, "late", (cb, h))
                bias(1, cb)
            for h in range(2):
                for q in range(2):
                    split_lo(nc.gpsimd, "cd_out", (h, q))

            with pool.Fori(0, NE // 2) as it:
                for w in range(2):
                    for s in range(33):
                        split_lo(nc.gpsimd, "moe", (w, s), it=it)
            pool.wait_ge(routed, 1)
            with pool.Fori(0, OVER) as j:
                more = pool.value_load(over_i[0:1, 0, bass.ds(j, 1)], min_val=0, max_val=NE)
                with pool.If(more > 0):
                    for s in range(33):
                        split_lo(nc.gpsimd, "over", (0, s), it=j)

        @block.scalar
        def _(act):
            chain = Count(act, act_chain)
            act.dma_start(sel[:], a["k_sel"]).then_inc(sel_in, 16)
            act.dma_start(X[:, 0:2, :], a["ctx"][0].rearrange("(t p) d -> p t d", p=P)).then_inc(x_in, 16)
            act.dma_start(X[:, 2:4, :], a["x"][0].rearrange("(t p) d -> p t d", p=P)).then_inc(x_in, 16)
            def splits(stage, *keys, it=0, size=SLAB):
                for key in keys:
                    split_hi(act, stage, key, size, it)

            nc.scalar.activation(cs[:], full(act, "start", "cT")[:, 0:16], ACT.Silu).then_inc(silu_c, 1)
            act.wait_ge(silu_c, 1)
            nc.scalar.activation(C4[:, :, 0:2], cs[:].rearrange("p (w k) -> p k w", w=2), ACT.Copy).then_inc(c_hi, 1)

            def gate(layer, cb, gate_of):
                st = ada_stage(layer, cb)
                for who in range(2 - layer):
                    b = full(act, st, ("bc", cb, who))
                    emptied(nc.scalar.activation(gate_of[who][:, cb // 6, (cb % 2) * 512:(cb % 2 + 1) * 512],
                                                 b[:], ACT.Copy), st, ("bc", cb, who))

            def roots(i, ready=None):
                tiles = NORM_TILES[i]
                for t in tiles:
                    if ready:
                        act.wait_ge(ready, len(tiles) + t - tiles[0] + 1)
                    nc.scalar.activation(xn_all(i, t), xt(i, t), ACT.Square, accum_out=ssq[:, t, 0:1]).then_inc(sumsq[i], 1)
                act.wait_ge(meansq[i], 1)
                nc.scalar.activation(root[:, tiles[0]:4, 0:1], rstd[:, tiles[0]:4, 0:1], ACT.Sqrt).then_inc(rooted[i], 1)

            def norm(i, layer, kinds):
                ht = norm_scratch(i)[1]
                for cb in range(3 * kinds, 3 * kinds + 4):
                    await_emptied(act, ada_stage(layer, cb), ("col", cb))
                for k in range(8):
                    b = full(act, f"norm{i}", k)
                    if i < 3 and k >= 2:
                        act.wait_ge(h_ready[i], k - 1)
                    for who in ((1, 0) if i < 3 else (0,)):
                        cols = slice(256 * (1 - who), 256 * (2 - who)) if i < 3 else slice(0, 256)
                        ins = nc.scalar.activation(ht[:, k % 2, cols] if i < 3 else h2T[:, k, :], b[:, cols], ACT.Identity,
                                                   scale=modcol[layer][:, kinds + 1, k, who:who + 1],
                                                   bias=modcol[layer][:, kinds, k, who:who + 1])
                        if who:
                            chain.mark(ins)
                    emptied(ins, f"norm{i}", k)

            splits("ada0", *[(cb, h) for cb in range(2) for h in range(2)])
            splits("ada0", (2, 0), (2, 1))
            act.wait_ge(x_in, 32)
            roots(0)
            splits("ada0", (3, 0), (3, 1))
            for dst, src in ((ws, a["a_w_s"][0].rearrange("g p q -> p g q")),
                             (wpool[:], a["b_w_pool"][0].rearrange("g i o -> i g o")),
                             (band[:], a["k_band"]), (vgain[:], a["a_v_gain"][0].partition_broadcast(P))):
                act.dma_start(dst, src).then_inc(ab_consts, 16)
            for dst, src in ((ropec[:], a["k_ropec"]), (roped[:], a["k_roped"]),
                             (q_gain[:], a["c_q_gain"][0].partition_broadcast(P)),
                             (k_gain[:], a["c_k_gain"][0].partition_broadcast(P))):
                act.dma_start(dst, src).then_inc(l1_in, 16)
            await_emptied(act, "start", "cT")

            def mix(n0, n1):
                for n_ in range(n0, n1):
                    splits(MIX_SLABS[n_][0], MIX_SLABS[n_][1])

            mix(0, 3)
            norm(0, 0, 0)
            for j in range(6):
                if j < 4:
                    for t in range(NT):
                        dst = (u if j < 2 else v)[:, t, (j % 2) * 256:(j % 2 + 1) * 256]
                        emptied(nc.scalar.activation(dst, full(act, "ab_in", (j, t))[:, 0:256], ACT.Gelu), "ab_in", (j, t))
                if j == 3:
                    for t in range(NT):
                        await_emptied(act, "ab_in", (3, t))
                        if t:
                            act.wait_ge(sumsq[4], t)
                        else:
                            await_emptied(act, "wsT", "wsT")
                        nc.scalar.activation(vsq, v[:, t, :], ACT.Square, accum_out=ssq[:, t, 1:2]).then_inc(sumsq[4], 1)
                mix(3 * j + 3, 3 * j + 6)
                if j == 3:
                    act.wait_ge(meansq[4], 1)
                    nc.scalar.activation(root[:, :, 1:2], rstd[:, :, 1:2], ACT.Sqrt).then_inc(rooted[4], 1)
                if j >= 1 and 3 + j in GATE_BLOCKS:
                    gate(0, 3 + j, gates)
            mix(21, 23)
            gate(0, 10, gates)
            mix(23, 25)
            act.wait_ge(ab_consts, 16 * 4)
            for g in range(4):
                b = full(act, "ab_yb", g)
                if g >= 2:
                    act.wait_ge(y_ready, g - 1)
                emptied(nc.scalar.activation(ybtmp[:, g % 2, :], b[:], ACT.Copy, scale=bscale_col[:, g:g + 1]), "ab_yb", g)
            mix(25, 26)
            gate(0, 11, gates)
            for g in range(4):
                nc.scalar.activation(Hhi[:, g, :], full(act, "ab_ya", g)[:], ACT.Copy).then_inc(ya_hi, 1)
            mix(26, 34)
            roots(1, x_ready[0])
            splits("ffn_in", "g0", "u0")
            norm(1, 0, 2)
            splits("ffn_in", "g1")

            def silu(i, first=False):
                for b in range(2):
                    if not first:
                        await_emptied(act, "ffn", ("u", b), i - 1)
                    src = full(act, "ffn", ("g", b), i)
                    emptied(nc.scalar.activation(sg[:, b, :], src[:], ACT.Silu), "ffn", ("g", b))

            def ffn_step(stage, keys, i, it=0):
                splits(stage, *keys[:2], it=it)
                silu(i)
                splits(stage, keys[2], it=it)
            act.wait_ge(h_ready[1], 8)
            silu(0, first=True)
            with act.Fori(0, 4) as it:
                for w in range(2):
                    ffn_step("ffn_loop", LOOP_KEYS[w], it * 2 + (1 + w), it)
            ffn_step("ffn_out", OUT_KEYS[0], 9)
            ffn_step("ffn_out", OUT_KEYS[1], 10)
            roots(2, x_ready[1])
            splits("cd_in", 0, 1, 2)
            norm(2, 1, 0)
            ahead = [("cd_in", 3), ("cd_in", 4), ("cd_in", 5), ("uq", 0), ("uq", 1), ("ukv", 0)]
            for j in range(6):
                for t in CD_TILES[j]:
                    width = min(256, CDIN - 256 * j)
                    dst = Zx[:, t - 2, 256 * j:256 * j + width] if t >= 2 else Zt[:, t, ZT0[j]:ZT0[j] + width]
                    emptied(nc.scalar.activation(dst, full(act, "cd_in", (j, t))[:, 0:width], ACT.Copy), "cd_in", (j, t))
                stage, key = ahead[j]
                splits(stage, key, size=slab_size(stage, key))
            await_emptied(act, "cd_in", (5, 3))
            act.wait_ge(ssq_clear, 1)
            for a_ in range(2):
                if a_:
                    chain.wait()
                chain.mark(nc.scalar.activation(pT[:, 0, 0:384], Zx[:, a_, CQ0:CKV0], ACT.Square, accum_out=ssq[:, 2 + a_, 10:11]))
            for t in range(NT):
                src = Zx[:, t - 2, CKV0:KR0] if t >= 2 else Zt[:, t, 384:640]
                if t:
                    act.wait_ge(sumsq[5], t)
                nc.scalar.activation(pT[:, 1, 0:256], src, ACT.Square, accum_out=ssq[:, t, 11:12]).then_inc(sumsq[5], 1)
            act.wait_ge(meansq[5], 1)
            nc.scalar.activation(root[:], rstd[:], ACT.Sqrt).then_inc(rooted[5], 1)
            act.wait_ge(l1_in, 16 * 4)
            for n_, (stage, b_, cols, col) in enumerate(COMPRESSED):
                src = full(act, stage, b_)
                if n_ >= 2:
                    act.wait_ge(cqn_ready, n_ - 1)
                gain = (cq_gain if stage == "cq" else ckv_gain)[:, b_:b_ + 1]
                emptied(nc.scalar.activation(X[:, 0, (n_ % 2) * 512:(n_ % 2) * 512 + cols], src[:, 0:cols], ACT.Copy,
                                             scale=gain), stage, b_)
            for h in range(2):
                for a_ in range(2):
                    emptied(nc.scalar.activation(qd[:, a_, 384 * h:384 * h + 384], full(act, "uq", (h, a_))[:, 0:384], ACT.Copy),
                            "uq", (h, a_))
            for stage, key in LATE_SLABS[0:2]:
                splits(stage, key)
            for t in range(NT):
                for h in range(2):
                    emptied(nc.scalar.activation(kv[:, t, 512 * h:512 * h + 512], full(act, "ukv", (t, h))[:], ACT.Copy),
                            "ukv", (t, h))
            splits(*LATE_SLABS[2])
            for h in range(8):
                emptied(nc.scalar.activation(kdT[0:64, h, :], full(act, "heads", ("kd", h))[0:64, :], ACT.Copy), "heads", ("kd", h))
            for i in range(34):
                if i < 32:
                    b = full(act, "att", ("s", i))
                    act.wait_ge(negmax, i + 1)
                    if i >= 2:
                        full(act, "att", ("t", i - 2))
                    emptied(nc.scalar.activation(pexp[:, i % 2, :], b[:], ACT.Exp, bias=rowmax[:, 1, i:i + 1],
                                                 scale=att_scale(i), accum_out=rowsum[:, 0, i:i + 1]), "att", ("s", i))
                if i % 4 == 1 and i > 4 and late_block(i - 5) in GATE_BLOCKS:
                    gate(1, late_block(i - 5), [gates1])
                if i < 32 and i % 2 == 0:
                    splits(*LATE_SLABS[i // 2 + 3])
            for b_ in range(4):
                nc.scalar.activation(oTh[:, 2 * b_:2 * b_ + 2, :], full(act, "oT", b_)[:], ACT.Copy).then_inc(oT_hi, 1)
            splits("cd_out", (1, 1))
            roots(3, x_ready[2])
            norm(3, 1, 2)
            for dst, src in ((ones[:], a["k_ones"]), (tri[:], a["k_tri"]), (slot_row[:], a["k_slot"]),
                             (expert_row[:], a["k_expert"]), (router[:], a["moe_router"][0].rearrange("(k p) e -> p k e", p=P))):
                act.dma_start(dst, src).then_inc(experts_in, 16)
            act.dma_start(fgain[:], a["final_gain"].partition_broadcast(P)).then_inc(fgain_in, 16)
            for b_ in range(4):
                nc.scalar.activation(h2h[:, b_ // 2, (b_ % 2) * 512:(b_ % 2 + 1) * 512],
                                     full(act, "route", ("back", b_))[:], ACT.Copy).then_inc(h2_hi, 1)
            act.wait_ge(logit_diff, 1)
            nc.scalar.activation(wts[:, :, 1:2], wts[:, :, 0:1], ACT.Exp).then_inc(gexp, 1)

            def gathered(stage, w, it=0):
                for h in range(2):
                    emptied(nc.scalar.activation(xgh[:, 4 * h:4 * h + 4, :], full(act, stage, ("xh", w, h), it)[:], ACT.Copy),
                            stage, ("xh", w, h))
                emptied(nc.scalar.activation(PT[:, 1 - w, :, :], full(act, stage, ("pt", w), it)[:, 0:256], ACT.Copy),
                        stage, ("pt", w))

            def silu_e(st, w, c, it):
                n_ = 512 if c < 5 else 256
                emptied(nc.scalar.activation(sge[:, c % 2, 0:n_], full(act, st, ("g", w, c), it)[:, 0:n_], ACT.Silu),
                        st, ("g", w, c))

            def act_hi(st, w, c, it):
                n_ = 4 if c < 5 else 2
                nc.scalar.activation(aTh[:, 4 * c:4 * c + n_, :], full(act, st, ("t", w, c), it)[:, 0:n_ * P],
                                     ACT.Copy).then_inc(hi_out[st == "over"], 1)

            def out_hi(st, w, it):
                for h in range(2):
                    nc.scalar.activation(yeh[:, h, :], full(act, st, ("d", w, h), it)[:], ACT.Copy).then_inc(hi_out[st == "over"], 1)

            def expert(st, w, it):
                for s in range(33):
                    split_hi(act, st, (w, s), it=it)
                    if w == 1 and s == 1:
                        out_hi(st, 0, it)
                    if s % 4 == 0 and 4 <= s <= 20:
                        silu_e(st, w, s // 4 - 1, it)
                    if s == 22:
                        silu_e(st, w, 5, it)
                    if s in (10, 14, 18, 22):
                        act_hi(st, w, (s - 10) // 4, it)
                    if s == 23:
                        act_hi(st, w, 4, it)
                    if s == 24:
                        if st == "moe":
                            gathered(st, w, it)
                        act_hi(st, w, 5, it)
            gathered("first", 1)
            with act.Fori(0, NE // 2) as it:
                expert("moe", 0, it)
                expert("moe", 1, it)
                out_hi("moe", 1, it)
            act.wait_ge(routed, 1)
            with act.Fori(0, OVER) as j:
                more = act.value_load(over_i[0:1, 0, bass.ds(j, 1)], min_val=0, max_val=NE)
                with act.If(more > 0):
                    gathered("over", 1, j)
                    expert("over", 0, j)
                    out_hi("over", 0, j)
            for t in range(2):
                act.wait_ge(y_done, t + 1)
                nc.scalar.activation(yM[:, t, :], X[:, 2 + t, :], ACT.Square, accum_out=ssq[:, t, 0:1]).then_inc(sumsq[6], 1)
            act.wait_ge(meansq[6], 1)
            nc.scalar.activation(root[:, 0:2, 0:1], rstd[:, 0:2, 0:1], ACT.Sqrt).then_inc(rooted[6], 1)

        @block.vector
        def _(dve):
            chain = Count(dve, dve_chain)
            V = nc.vector

            def splits(stage, *keys, it=0, size=SLAB):
                for key in keys:
                    split_lo(V, stage, key, size, it)

            def hi_lo(dst_hi, dst_lo, src, ready):
                chain.mark(V.tensor_copy(dst_hi, src))
                chain.wait()
                V.tensor_tensor(dst_lo, src, dst_hi.bitcast(F32), ALU.subtract).then_inc(ready, 1)

            def inverse_root(i, parts):
                for p_, (dst, src, n_) in enumerate(parts):
                    ins = V.tensor_scalar(dst, src, 1.0 / n_, EPS, ALU.mult, ALU.add)
                    if p_ < len(parts) - 1:
                        chain.mark(ins)
                ins.then_inc(meansq[i], 1)
                dve.wait_ge(rooted[i], 1)

            def normalise(i):
                tiles = NORM_TILES[i]
                dve.wait_ge(sumsq[i], len(tiles))
                cols = (slice(None), slice(tiles[0], 4), slice(0, 1))
                inverse_root(i, [(rstd[cols], ssq[cols], D)])
                chain.mark(V.reciprocal(rstd[cols], root[cols]))
                chain.wait()
                for t in tiles:
                    V.tensor_scalar(xn_all(i, t), xt(i, t), rstd[:, t, 0:1], None, ALU.mult).then_inc(xn_ready[i], 1)

            def norm(i):
                for k in range(8):
                    await_emptied(dve, f"norm{i}", k)
                    hi_lo(H_of(i)[0][:, k, :], H_of(i)[1][:, k, :], norm_scratch(i)[1][:, k % 2, :], h_ready[i])

            def residual(stage, key, n_, t, gate, tmp, ready):
                h = key[0]
                cols = slice(512 * h, 512 * h + 512)
                b = full(dve, stage, key)
                if n_ >= 2:
                    dve.wait_ge(ready, n_ - 1)
                emptied(V.tensor_tensor(tmp, b[:], gate[:, cols], ALU.mult), stage, key)
                await_emptied(dve, stage, key)
                V.tensor_tensor(X[:, t, cols], X[:, t, cols], tmp, ALU.add).then_inc(ready, 1)

            dve.wait_ge(silu_c, 1)
            emptied(V.tensor_copy(pcols[:], full(dve, "start", "cT")[:, 16:29]), "start", "cT")
            dve.wait_ge(c_hi, 1)
            V.tensor_tensor(C4[:, :, 2:4], cs[:].rearrange("p (w k) -> p k w", w=2), C4[:, :, 0:2].bitcast(F32),
                            ALU.subtract).then_inc(c_lo, 1)

            def mod_row(layer, cb):
                st = ada_stage(layer, cb)
                b = full(dve, st, ("m", cb))
                if st == "late":
                    if cb > LATE[0]:
                        full(dve, st, spread(cb - 1))
                elif before(layer, cb):
                    full(dve, *before(layer, cb))
                emptied(V.tensor_copy(mod_rows(st, cb)[0:4], b[0:4, :]), st, ("m", cb))

            def mod_col(layer, cb):
                kind, st = KIND[cb // 2], ada_stage(layer, cb)
                b = full(dve, st, ("col", cb))[:, 0:8].rearrange("p (j w) -> p j w", w=2)
                emptied(V.tensor_scalar(modcol[layer][:, kind, (cb % 2) * 4:(cb % 2 + 1) * 4, :], b, float(kind % 2),
                                        None, ALU.add), st, ("col", cb))

            def mix(n0, n1):
                for n_ in range(n0, n1):
                    splits(MIX_SLABS[n_][0], MIX_SLABS[n_][1])

            for cb in range(4):
                if cb == 3:
                    normalise(0)
                splits("ada0", (cb, 0), (cb, 1))
                if cb >= 1:
                    mod_row(0, cb - 1)
                if cb >= 2:
                    mod_col(0, cb - 2)
            mod_row(0, 3)
            mod_col(0, 2)
            mod_col(0, 3)
            mix(0, 3)
            norm(0)
            await_emptied(dve, "start", "cT")
            dve.wait_ge(ab_consts, 16 * 4)
            emptied(V.tensor_copy(wsT[:], full(dve, "wsT", "wsT")[:]), "wsT", "wsT")
            await_emptied(dve, "wsT", "wsT")
            for j in range(6):
                if j >= 4:
                    for t in range(NT):
                        b = full(dve, "ab_in", (j, t))
                        emptied(V.tensor_copy(zp[:, t, (j - 4) * 256:(j - 3) * 256], b[:, 0:256]), "ab_in", (j, t))
                mix(3 * j + 3, 3 * j + 6)
                mod_row(0, 4 + j)
                if j >= 1 and 3 + j not in GATE_BLOCKS:
                    mod_col(0, 3 + j)
                if j == 3:
                    dve.wait_ge(sumsq[4], NT)
                    inverse_root(4, [(rstd[:, :, 1:2], ssq[:, :, 1:2], AW)])
                    chain.mark(V.reciprocal(rstd[:, :, 1:2], root[:, :, 1:2]))
                    chain.wait()
                    for t in range(NT):
                        V.scalar_tensor_tensor(out=v[:, t, :], in0=v[:, t, :], scalar=rstd[:, t, 1:2], in1=vgain[:],
                                               op0=ALU.mult, op1=ALU.mult).then_inc(v_ready, 1)
            mix(21, 22)
            mod_row(0, 10)
            mod_col(0, 9)
            mix(22, 24)
            mod_row(0, 11)
            mix(24, 25)
            for t in range(NT):
                b = full(dve, "ab_s", t)
                for g in range(4):
                    cols = slice(g * P, (g + 1) * P)
                    ins = V.scalar_tensor_tensor(out=u[:, t, cols], in0=b[:, cols], scalar=bs_col[:, g:g + 1], in1=u[:, t, cols],
                                                 op0=ALU.add, op1=ALU.mult)
                    if g < 3:
                        chain.mark(ins)
                emptied(ins, "ab_s", t)

            def pooled(g):
                b = full(dve, "ab_pool", g)
                if g >= 2:
                    full(dve, "ab_yb", g - 2)
                emptied(V.tensor_copy(pooledT[:, g % 2, :], b[:]), "ab_pool", g)

            def yb(g):
                await_emptied(dve, "ab_yb", g)
                hi_lo(Hhi[:, 4 + g, :], Hlo[:, 4 + g, :], ybtmp[:, g % 2, :], y_ready)
            pooled(0)
            for g in range(4):
                if g < 3:
                    pooled(g + 1)
                yb(g)
            mix(25, 26)
            mod_row(1, 0)
            for g in range(4):
                b = full(dve, "ab_ya", g)
                dve.wait_ge(ya_hi, g + 1)
                emptied(V.tensor_tensor(Hlo[:, g, :], b[:], Hhi[:, g, :].bitcast(F32), ALU.subtract), "ab_ya", g)
            mix(26, 29)
            mod_row(1, 1)
            mod_col(1, 0)
            mix(29, 31)
            for t in range(NT):
                residual("ab_out", (0, t), t, t, gates[int(t < 2)][:, 0, :], u[:, t % 2, :], x_ready[0])
            mix(31, 33)
            for t in range(NT):
                residual("ab_out", (1, t), 4 + t, t, gates[int(t < 2)][:, 0, :], u[:, t % 2, :], x_ready[0])
            mix(33, 34)
            mod_row(1, 2)
            mod_col(1, 1)
            mod_row(1, 3)
            mod_col(1, 2)
            mod_col(1, 3)
            normalise(1)
            splits("ffn_in", "g0", "u0")
            norm(1)
            splits("ffn_in", "g1")

            def hidden(i, parity):
                for b_ in range(2):
                    await_emptied(dve, "ffn", ("g", b_), i)
                    b = full(dve, "ffn", ("u", b_), i)
                    emptied(V.tensor_tensor(am[:, b_, :], b[:], sg[:, b_, :], ALU.mult), "ffn", ("u", b_))
                for b_ in range(2):
                    await_emptied(dve, "ffn", ("u", b_), i)
                    ins = V.tensor_copy(acth[:, parity, b_, :], am[:, b_, :])
                    chain.mark(ins)
                chain.wait()
                for b_ in range(2):
                    V.tensor_tensor(actl[:, parity, b_, :], am[:, b_, :], acth[:, parity, b_, :].bitcast(F32),
                                    ALU.subtract).then_inc(ff_ready, 1)

            def add_down(i, outs, first=False):
                for o in outs:
                    t, h = o % 4, o // 4
                    b = full(dve, "ffn", ("d", o), i)
                    y = yacc[:, t, 512 * h:512 * h + 512]
                    if first:
                        emptied(V.tensor_copy(y, b[:]), "ffn", ("d", o))
                    else:
                        emptied(V.tensor_tensor(y, y, b[:], ALU.add), "ffn", ("d", o))

            def ffn_step(stage, keys, i, parity, it=0, first=False):
                splits(stage, *keys[:2], it=it)
                hidden(i, parity)
                add_down(i - 1, range(4), first)
                splits(stage, keys[2], it=it)
                add_down(i - 1, range(4, 8), first)
            hidden(0, 0)
            dve.wait_ge(ff_ready, 2)
            chain.mark(V.memset(yacc[:], 0.0))
            chain.wait()
            with dve.Fori(0, 4) as it:
                chain.enter(it, 4)
                for w in range(2):
                    ffn_step("ffn_loop", LOOP_KEYS[w], it * 2 + (1 + w), 1 - w, it)
                chain.leave(4)
            ffn_step("ffn_out", OUT_KEYS[0], 9, 1)
            ffn_step("ffn_out", OUT_KEYS[1], 10, 0)
            for o in range(8):
                t, cols = o % 4, slice(512 * (o // 4), 512 * (o // 4) + 512)
                add_down(10, [o])
                await_emptied(dve, "ffn", ("d", o), 10)
                chain.mark(V.tensor_tensor(yacc[:, t, cols], yacc[:, t, cols], gates[int(t < 2)][:, 1, cols], ALU.mult))
                chain.wait()
                V.tensor_tensor(X[:, t, cols], X[:, t, cols], yacc[:, t, cols], ALU.add).then_inc(x_ready[1], 1)
            normalise(2)
            splits("cd_in", 0, 1, 2)
            norm(2)
            V.memset(ssq[:], 1.0).then_inc(ssq_clear, 1)
            dve.wait_ge(ssq_clear, 1)
            ahead = [("cd_in", 3), ("cd_in", 4), ("cd_in", 5), ("uq", 0), ("uq", 1), ("ukv", 0)]

            def heads(x, n_, d=64):
                return x.rearrange("p (h d) -> p h d", h=n_)
            sq = pexp[:].rearrange("p a b -> p (a b)")
            for j in range(6):
                await_emptied(dve, "cd_in", (j, 3))
                stage, key = ahead[j]
                splits(stage, key, size=slab_size(stage, key))
                if j == 2:
                    for t in range(NT):
                        src, h0 = (Zx[:, t - 2, 0:640], 0) if t >= 2 else (Zt[:, t, 0:128], 8)
                        n_ = (10 - h0) * 64
                        chain.wait()
                        chain.mark(V.tensor_tensor(sq[:, 0:n_], src, src, ALU.mult))
                        chain.wait()
                        chain.mark(V.tensor_reduce(ssq[:, t, h0:10], heads(sq[:, 0:n_], 10 - h0), AX, ALU.add))
            dve.wait_ge(l1_in, 16 * 4)
            dve.wait_ge(sumsq[5], NT)
            chain.wait()
            inverse_root(5, [(rstd[:, :, 0:10], ssq[:, :, 0:10], 64), (rstd[:, :, 10:11], ssq[:, :, 10:11], 384),
                             (rstd[:, :, 11:12], ssq[:, :, 11:12], 256)])
            chain.mark(V.reciprocal(rstd[:], root[:]))
            chain.wait()
            for a_ in range(2):
                V.tensor_scalar(Zx[:, a_, CQ0:CKV0], Zx[:, a_, CQ0:CKV0], rstd[:, 2 + a_, 10:11], None, ALU.mult).then_inc(cn_ready, 1)
            for t in range(NT):
                x = Zx[:, t - 2, CKV0:KR0] if t >= 2 else Zt[:, t, 384:640]
                V.tensor_scalar(x, x, rstd[:, t, 11:12], None, ALU.mult).then_inc(cn_ready, 1)
            for n_, (stage, b_, cols, col) in enumerate(COMPRESSED):
                await_emptied(dve, stage, b_)
                hi_lo(H1hi[:, col, 0:cols], H1lo[:, col, 0:cols], X[:, 0, (n_ % 2) * 512:(n_ % 2) * 512 + cols], cqn_ready)

            def rope(x, tmp, table, a_, n_, half):
                s = table[:, a_, 1, :].unsqueeze(1).to_broadcast([P, n_, 2 * half])
                c = table[:, a_, 0, :].unsqueeze(1).to_broadcast([P, n_, 2 * half])
                chain.wait()
                chain.mark(V.tensor_tensor(tmp[:, :, 0:half], x[:, :, half:2 * half], s[:, :, 0:half], ALU.mult))
                chain.mark(V.tensor_tensor(tmp[:, :, half:2 * half], x[:, :, 0:half], s[:, :, half:2 * half], ALU.mult))
                chain.wait()
                chain.mark(V.tensor_tensor(x, x, c, ALU.mult))
                chain.wait()
            for t in range(NT):
                if t < 2:
                    k_ = heads(Zt[:, t, 0:128], 2)
                else:
                    x10 = heads(Zx[:, t - 2, 0:640], 10)
                    q_, k_ = x10[:, 0:8, :], x10[:, 8:10, :]
                    chain.mark(V.tensor_tensor(q_, q_, rstd[:, t, 0:8].unsqueeze(2).to_broadcast([P, 8, 64]), ALU.mult))
                    chain.wait()
                    chain.mark(V.tensor_tensor(q_, q_, q_gain[:].unsqueeze(1).to_broadcast([P, 8, 64]), ALU.mult))
                chain.mark(V.tensor_tensor(k_, k_, rstd[:, t, 8:10].unsqueeze(2).to_broadcast([P, 2, 64]), ALU.mult))
                chain.wait()
                ins = V.tensor_tensor(k_, k_, k_gain[:].unsqueeze(1).to_broadcast([P, 2, 64]), ALU.mult)
                if t < 2:
                    ins.then_inc(qk_ready, 1)
                    continue
                chain.mark(ins)
                tmp = heads(sq[:, 0:640], 10)
                rope(x10, tmp, ropec, t - 2, 10, 32)
                chain.mark(V.tensor_tensor(tmp, tmp, x10, ALU.add))
                chain.wait()
                chain.mark(V.tensor_copy(Zx[:, t - 2, 0:512].rearrange("p (j g d) -> p g j d", j=4, g=2),
                                         sq[:, 0:512].rearrange("p (g j d) -> p g j d", g=2, j=4)))
                V.tensor_copy(Zx[:, t - 2, 512:640], sq[:, 512:640]).then_inc(qk_ready, 1)
                kr = Zx[:, t - 2, KR0:CDIN].unsqueeze(1)
                dve.wait_ge(qk_ready, t + 1)
                tmp = sq[:, 640:672].unsqueeze(1)
                rope(kr, tmp, roped, t - 2, 1, 16)
                V.tensor_tensor(kr, kr, tmp, ALU.add).then_inc(kr_ready, 1)
            for stage, key in LATE_SLABS[0:2]:
                splits(stage, key)
            for a_ in range(2):
                for h in range(2):
                    await_emptied(dve, "uq", (h, a_))
                x = qd[:, a_, :].rearrange("p (h d) -> p h d", h=8)[:, :, 64:96]
                tmp = sq[:, 0:256].rearrange("p (h d) -> p h d", h=8)
                rope(x, tmp, roped, a_, 8, 16)
                V.tensor_tensor(x, x, tmp, ALU.add).then_inc(rope_ready, 1)
                dve.wait_ge(rope_ready, a_ + 1)
            splits(*LATE_SLABS[2])
            emptied(V.tensor_copy(kcT[:], full(dve, "heads", "kc")[:]), "heads", "kc")
            for i in range(2):
                b = full(dve, "heads", ("qc", i))
                emptied(V.tensor_copy(qcT[:, 2 * i:2 * i + 2, :], b[:].rearrange("p (j t) -> p j t", j=2)), "heads", ("qc", i))
            b = full(dve, "heads", "kr")
            emptied(V.tensor_copy(kdT[64:96, :, :], b[0:32, :].unsqueeze(1).to_broadcast([32, 8, 512])), "heads", "kr")
            for i in range(4):
                b = full(dve, "heads", ("qd", i))
                emptied(V.tensor_copy(qdT[0:96, 2 * i:2 * i + 2, :], b[0:96, :].rearrange("p (j t) -> p j t", j=2)), "heads", ("qd", i))

            for i in range(34):
                if i < 32:
                    b = full(dve, "att", ("s", i))
                    chain.mark(V.reduce_max(rowmax[:, 0, i:i + 1], b[:], AX))
                    chain.wait()
                    V.tensor_scalar(rowmax[:, 1, i:i + 1], rowmax[:, 0, i:i + 1], -att_scale(i), None, ALU.mult).then_inc(negmax, 1)
                if 2 <= i:
                    br, h, a_ = unit(i - 2)
                    await_emptied(dve, "att", ("s", i - 2))
                    chain.mark(V.reciprocal(rowsum[:, 1, i - 2:i - 1], rowsum[:, 0, i - 2:i - 1]))
                    chain.wait()
                    b = full(dve, "att", ("o", i - 2))
                    c0 = br * 512 + h * 64
                    emptied(V.tensor_scalar(X[:, a_, c0:c0 + 64], b[:, 0:64], rowsum[:, 1, i - 2:i - 1], None, ALU.mult),
                            "att", ("o", i - 2))
                if 1 <= i < 33:
                    b = full(dve, "att", ("t", i - 1))
                    if i >= 3:
                        full(dve, "att", ("o", i - 3))
                    emptied(V.tensor_copy(pT[:, (i - 1) % 2, :], b[:]), "att", ("t", i - 1))
                if i % 4 == 1 and i > 4 and late_block(i - 5) not in GATE_BLOCKS:
                    mod_col(1, late_block(i - 5))
                if i < 32 and i % 4 == 2:
                    mod_row(1, late_block(i - 2))
                if i < 32 and i % 2 == 0:
                    splits(*LATE_SLABS[i // 2 + 3])
            for b_ in range(4):
                b = full(dve, "oT", b_)
                dve.wait_ge(oT_hi, b_ + 1)
                emptied(V.tensor_tensor(oTl[:, 2 * b_:2 * b_ + 2, :], b[:].rearrange("p (j t) -> p j t", j=2),
                                        oTh[:, 2 * b_:2 * b_ + 2, :].bitcast(F32), ALU.subtract), "oT", b_)
            splits("cd_out", (1, 1))
            for h in range(2):
                for a_ in range(2):
                    residual("cd_out", (h, a_), 2 * h + a_, 2 + a_, gates1[:, 0, :], pexp[:, a_, :], x_ready[2])
            normalise(3)
            chain.mark(V.memset(yM, 0.0))
            chain.mark(V.memset(posn[:], -1.0))
            chain.wait()
            for b_ in range(4):
                b = full(dve, "route", ("back", b_))
                dve.wait_ge(h2_hi, b_ + 1)
                cols = slice((b_ % 2) * 512, (b_ % 2 + 1) * 512)
                emptied(V.tensor_tensor(h2l[:, b_ // 2, cols], b[:], h2h[:, b_ // 2, cols].bitcast(F32), ALU.subtract),
                        "route", ("back", b_))
            emptied(V.tensor_copy(logits[:], full(dve, "route", "logits")[:, 0:16].rearrange("p (t e) -> p t e", t=2)), "route", "logits")
            await_emptied(dve, "route", "logits")
            dve.wait_ge(experts_in, 16 * 5)
            for t in range(2):
                chain.mark(V.max(top[:, t, :], logits[:, t, :]))
                chain.wait()
                chain.mark(V.max_index(topi[:, t, :], top[:, t, :], logits[:, t, :]))
                chain.wait()
                chain.mark(V.tensor_copy(topf[:, t, :], topi[:, t, :]))
                chain.wait()
                for j in range(2):
                    chain.mark(V.tensor_scalar(pick[:, t, j, :], expert_row[:], topf[:, t, j:j + 1], None, ALU.is_equal))
                chain.wait()
                V.tensor_tensor(chosen[:, t, :], pick[:, t, 0, :], pick[:, t, 1, :], ALU.add).then_inc(chosen_ready, 1)
            V.tensor_tensor(wts[:, :, 0:1], top[:, :, 1:2], top[:, :, 0:1], ALU.subtract).then_inc(logit_diff, 1)
            dve.wait_ge(gexp, 1)
            chain.mark(V.tensor_scalar(wts[:, :, 2:3], wts[:, :, 1:2], 1.0, None, ALU.add))
            chain.wait()
            chain.mark(V.reciprocal(wts[:, :, 2:3], wts[:, :, 2:3]))
            chain.wait()
            chain.mark(V.tensor_tensor(wts[:, :, 3:4], wts[:, :, 1:2], wts[:, :, 2:3], ALU.mult))
            chain.wait()
            for t in range(2):
                chain.mark(V.tensor_scalar(gate_e[:, t, :], pick[:, t, 0, :], wts[:, t, 2:3], None, ALU.mult))
                chain.wait()
                chain.mark(V.scalar_tensor_tensor(out=gate_e[:, t, :], in0=pick[:, t, 1, :], scalar=wts[:, t, 3:4],
                                                  in1=gate_e[:, t, :], op0=ALU.mult, op1=ALU.add))
            b = full(dve, "route", "cum")
            dve.wait_ge(chosen_ready, 2)
            chain.mark(V.tensor_tensor(posn[:, :, 0:NE], b[:, 0:16].rearrange("p (t e) -> p t e", t=2), chosen[:], ALU.mult))
            chain.wait()
            chain.mark(V.tensor_scalar(posn[:, :, 0:NE], posn[:, :, 0:NE], -1.0, None, ALU.add))
            emptied(V.tensor_scalar(over[:, 0, :], b[:, 16:24], CAP + 0.5, None, ALU.is_gt), "route", "cum")
            chain.mark(V.tensor_scalar(over[:, 1, :], expert_row[:], -1.0, float(NE), ALU.mult, ALU.add))
            chain.wait()
            await_emptied(dve, "route", "cum")
            chain.mark(V.tensor_tensor(over[:, 0, :], over[:, 0, :], over[:, 1, :], ALU.mult))
            chain.wait()
            chain.mark(V.max(over[:, 2, :], over[:, 0, :]))
            chain.wait()
            chain.mark(V.tensor_scalar(over[:, 1, :], over[:, 2, :], -1.0, float(NE), ALU.mult, ALU.add))
            chain.wait()
            chain.mark(V.tensor_scalar(over_i[:, 1, :], over[:, 1, :], float(NE - 1), None, ALU.min))
            V.tensor_copy(over_i[:, 0, :], over[:, 2, :]).then_inc(routed, 1)

            def place(r, par, e):
                for t in range(2):
                    V.tensor_scalar(Pm[:, par, t, :], slot_row[:, r * SLOTS:(r + 1) * SLOTS], posn[:, t, bass.ds(e, 1)], None,
                                    ALU.is_equal).then_inc(p_ready[r], 1)

            def gathered_lo(stage, w, it=0):
                for h in range(2):
                    emptied(V.tensor_copy(xgl[:, 4 * h:4 * h + 4, :], full(dve, stage, ("xl", w, h), it)[:]
                                          .rearrange("p (k s) -> p k s", k=4)), stage, ("xl", w, h))

            def act_e(st, w, c, it):
                n_ = 512 if c < 5 else 256
                await_emptied(dve, st, ("g", w, c), it)
                b = full(dve, st, ("u", w, c), it)
                emptied(V.tensor_tensor(ame[:, c % 2, 0:n_], b[:, 0:n_], sge[:, c % 2, 0:n_], ALU.mult), st, ("u", w, c))

            def hi_there(st, i, it):
                dve.wait_ge(hi_out[st == "over"], it * (8 if st == "over" else 16) + (i + 1))

            def act_lo(st, w, c, it):
                n_ = 4 if c < 5 else 2
                b = full(dve, st, ("t", w, c), it)
                hi_there(st, 8 * w + c, it)
                emptied(V.tensor_tensor(aTl[:, 4 * c:4 * c + n_, :], b[:, 0:n_ * P].rearrange("p (k s) -> p k s", k=n_),
                                        aTh[:, 4 * c:4 * c + n_, :].bitcast(F32), ALU.subtract), st, ("t", w, c))

            def out_lo(st, w, it):
                for h in range(2):
                    b = full(dve, st, ("d", w, h), it)
                    hi_there(st, 8 * w + 6 + h, it)
                    emptied(V.tensor_tensor(yel[:, h, :], b[:], yeh[:, h, :].bitcast(F32), ALU.subtract), st, ("d", w, h))

            def add_out(st, w, e, it):
                for o in range(4):
                    t, h = o // 2, o % 2
                    b = full(dve, st, ("y", w, o), it)
                    y = yM[:, t, 512 * h:512 * h + 512]
                    emptied(V.scalar_tensor_tensor(out=y, in0=b[:], scalar=gate_e[:, t, bass.ds(e, 1)], in1=y,
                                                   op0=ALU.mult, op1=ALU.add), st, ("y", w, o))

            def expert(st, w, it):
                for s in range(33):
                    splits(st, (w, s), it=it)
                    if w == 1 and s == 1:
                        out_lo(st, 0, it)
                    if w == 1 and s == 5:
                        add_out(st, 0, it * 2, it)
                    if s in (6, 10, 14, 18, 22):
                        act_e(st, w, (s - 6) // 4, it)
                    if s in (10, 14, 18, 22):
                        act_lo(st, w, (s - 10) // 4, it)
                    if s == 12 and st == "moe":
                        place(0, 1 - w, it * 2 + (w + 1))
                    if s == 23:
                        act_e(st, w, 5, it)
                        act_lo(st, w, 4, it)
                    if s == 24:
                        if st == "moe":
                            gathered_lo(st, w, it)
                        act_lo(st, w, 5, it)
            place(0, 0, 0)
            gathered_lo("first", 1)
            with dve.Fori(0, NE // 2) as it:
                expert("moe", 0, it)
                expert("moe", 1, it)
                out_lo("moe", 1, it)
                add_out("moe", 1, it * 2 + 1, it)
            for o in (2, 3):
                await_emptied(dve, "moe", ("y", 1, o), NE // 2 - 1)
            dve.wait_ge(routed, 1)
            V.tensor_copy(over[:, 0, 0:1], over[:, 2, 0:1]).then_inc(summed, 1)
            with dve.Fori(0, OVER) as j:
                more = dve.value_load(over_i[0:1, 0, bass.ds(j, 1)], min_val=0, max_val=NE)
                with dve.If(more > 0):
                    e = dve.value_load(over_i[0:1, 1, bass.ds(j, 1)], min_val=0, max_val=NE - 1)
                    dve.wait_ge(summed, j + 1)
                    place(1, 0, e)
                    gathered_lo("over", 1, j)
                    expert("over", 0, j)
                    out_lo("over", 0, j)
                    add_out("over", 0, e, j)
                    for o in (2, 3):
                        await_emptied(dve, "over", ("y", 0, o), j)
                    V.tensor_copy(over[:, 0, 0:1], over[:, 2, 0:1]).then_inc(summed, 1)
            dve.wait_ge(fgain_in, 16)
            for t in range(2):
                chain.mark(V.tensor_tensor(yM[:, t, :], yM[:, t, :], gates1[:, 1, :], ALU.mult))
            chain.wait()
            for t in range(2):
                V.tensor_tensor(X[:, 2 + t, :], X[:, 2 + t, :], yM[:, t, :], ALU.add).then_inc(y_done, 1)
            dve.wait_ge(sumsq[6], 2)
            inverse_root(6, [(rstd[:, 0:2, 0:1], ssq[:, 0:2, 0:1], D)])
            chain.mark(V.reciprocal(rstd[:, 0:2, 0:1], root[:, 0:2, 0:1]))
            chain.wait()
            for t in range(2):
                V.scalar_tensor_tensor(out=yM[:, t, :], in0=X[:, 2 + t, :], scalar=rstd[:, t, 0:1], in1=fgain[:],
                                       op0=ALU.mult, op1=ALU.mult).then_inc(fin_ready, 1)

        @block.tensor
        def _(pe):
            T = nc.tensor

            def used(ins):
                ins.then_inc(slab_used, 1)

            def columns_of(layer, cb):
                st = ada_stage(layer, cb)
                await_emptied(pe, st, ("m", cb))
                if layer == 0 and cb < 4:
                    pe.wait_ge(first_bias_in, 16 * 4)
                else:
                    pe.wait_ge(bias_in[cb % 2], 16 * (6 * layer + cb // 2 - 1))
                row = mod_rows(st, cb)
                if cb in GATE_BLOCKS:
                    for who in range(2 - layer):
                        filled(T.matmul(bank(pe, st, ("bc", cb, who))[:], sel[:, who, :], row, start=True, stop=True),
                               st, ("bc", cb, who))
                    return
                b = bank(pe, st, ("col", cb))
                for j in range(4):
                    ins = T.matmul(b[:, 2 * j:2 * j + 2], row[:, j * P:(j + 1) * P], sel[:, :, 0], start=True, stop=True)
                filled(ins, st, ("col", cb))

            def rows_of(layer, cb, h):
                st = ada_stage(layer, cb)
                b = bank(pe, st, ("m", cb)) if h == 0 else ps[banks[st, ("m", cb)][0]]
                wh, wl = slab(pe, st, (cb, h), (4, 512))
                for k in range(4):
                    T.matmul(b[0:4, :], C4[:, 4 * h + k, :], wh[:, k, :], start=(h == 0 and k == 0), stop=False)
                    ins = T.matmul(b[0:4, :], C4[:, 4 * h + k, :], wl[:, k, :], start=False, stop=(h == 1 and k == 3))
                used(ins)

            def rows_of_block(layer, cb):
                for h in range(2):
                    rows_of(layer, cb, h)

            def norm(i):
                tiles = NORM_TILES[i]
                pe.wait_ge(xn_ready[i], len(tiles))
                for k in range(8):
                    b = bank(pe, f"norm{i}", k)
                    for n_, t in enumerate(tiles):
                        ins = T.transpose(b[:, n_ * P:(n_ + 1) * P], xn_block(i, t, k), ident[:])
                    filled(ins, f"norm{i}", k)

            def project(stage, keys, blocks, tiles, left, bank_of, ready=None):
                k0 = 0
                for s_, (key, width) in enumerate(keys):
                    wh, wl = slab(pe, stage, key, (blocks, width))
                    for t in tiles:
                        b = bank(pe, stage, bank_of(t)) if s_ == 0 else ps[banks[stage, bank_of(t)][0]]
                        for k in range(blocks):
                            if ready and t == tiles[0]:
                                pe.wait_ge(ready, k + 1)
                            lh, ll = left(k0 + k, t)
                            ins = product(pe, b[:, 0:width], lh, ll, wh[:, k, :], wl[:, k, :], s_ == 0 and k == 0,
                                          s_ == len(keys) - 1 and k == blocks - 1)
                        if s_ == len(keys) - 1 and t != tiles[-1]:
                            filled(ins, stage, bank_of(t))
                    used(ins)
                    k0 += blocks

            def tok(hh, hl):
                return lambda k, t: (hh[:, k, t * P:(t + 1) * P], hl[:, k, t * P:(t + 1) * P])

            pe.wait_ge(ident_in, 16)
            pe.wait_ge(c_in, 16 * 6)
            filled(T.transpose(bank(pe, "start", "cT")[:, 0:29], crows[:], ident[0:29, 0:29]), "start", "cT")
            pe.wait_ge(c_lo, 1)
            pe.wait_ge(sel_in, 16)
            for cb in range(4):
                rows_of_block(0, cb)
                if cb >= 1:
                    columns_of(0, cb - 1)
            columns_of(0, 3)
            norm(0)
            pe.wait_ge(ab_consts, 16 * 4)
            b = bank(pe, "wsT", "wsT")
            for g in range(4):
                ins = T.transpose(b[:, g * P:(g + 1) * P], ws[:, g, :], ident[:])
            filled(ins, "wsT", "wsT")
            for j in range(6):
                project("ab_in", [(j, 256)], 8, range(4), tok(Hhi, Hlo), lambda t: (j, t), None if j else h_ready[0])
                rows_of_block(0, 4 + j)
                if j >= 1:
                    columns_of(0, 3 + j)
            rows_of_block(0, 10)
            columns_of(0, 9)
            rows_of_block(0, 11)
            columns_of(0, 10)
            for t in range(NT):
                pe.wait_ge(v_ready, t + 1)
                b = bank(pe, "ab_s", t)
                for g in range(4):
                    ins = T.matmul(b[:, g * P:(g + 1) * P], wsT[:, g, :], v[:, t, g * P:(g + 1) * P], start=True, stop=True)
                filled(ins, "ab_s", t)

            def pool(g):
                await_emptied(pe, "ab_in", (4 + g // 2, 3))
                b = bank(pe, "ab_pool", g)
                for s_ in range(2):
                    for a_ in range(2):
                        c0 = 256 * s_ + 112 * a_
                        ins = T.matmul(b[:, c0:c0 + 144], zp[:, 2 * s_ + a_, g * P:(g + 1) * P], band[:, g, a_, :],
                                       start=(s_ == 0 and a_ == 0), stop=(s_ == 1 and a_ == 1), skip_group_check=True)
                filled(ins, "ab_pool", g)

            def yb(g):
                await_emptied(pe, "ab_pool", g)
                filled(T.matmul(bank(pe, "ab_yb", g)[:], wpool[:, g, :], pooledT[:, g % 2, :], start=True, stop=True), "ab_yb", g)
            pool(0)
            for g in range(4):
                if g < 3:
                    pool(g + 1)
                yb(g)
            rows_of_block(1, 0)
            columns_of(0, 11)
            for g in range(4):
                b = bank(pe, "ab_ya", g)
                for t in range(NT):
                    await_emptied(pe, "ab_s", t)
                    ins = T.transpose(b[:, t * P:(t + 1) * P], u[:, t, g * P:(g + 1) * P], ident[:])
                filled(ins, "ab_ya", g)
            rows_of_block(1, 1)
            columns_of(1, 0)
            pe.wait_ge(y_ready, 4)
            for g in range(4):
                await_emptied(pe, "ab_ya", g)
            for h in range(2):
                project("ab_out", [((h, 0), 512), ((h, 1), 512)], 4, range(4), tok(Hhi, Hlo), lambda t: (h, t))
            rows_of_block(1, 2)
            columns_of(1, 1)
            rows_of_block(1, 3)
            columns_of(1, 2)
            columns_of(1, 3)
            norm(1)

            def hidden(kind, stage, key, i, it=0):
                wh, wl = slab(pe, stage, key, (8, 256), it)
                for b_ in range(2):
                    b = bank(pe, "ffn", (kind, b_), i)
                    for k in range(KD):
                        if stage == "ffn_in" and key == "g0" and b_ == 0:
                            pe.wait_ge(h_ready[1], k + 1)
                        cols = slice(b_ * P, (b_ + 1) * P)
                        ins = product(pe, b[:], wh[:, k, cols], wl[:, k, cols], Hhi[:, k, :], Hlo[:, k, :], k == 0, k == KD - 1)
                    if b_ == 0:
                        filled(ins, "ffn", (kind, b_))
                used(ins)

            def down(stage, key, i, parity, it=0):
                pe.wait_ge(ff_ready, i * 2 + 2)
                wh, wl = slab(pe, stage, key, (2, D), it)
                for o in range(8):
                    t, h = o % 4, o // 4
                    b = bank(pe, "ffn", ("d", o), i)
                    for k in range(2):
                        cols, toks = slice(512 * h, 512 * h + 512), slice(t * P, (t + 1) * P)
                        ins = product(pe, b[:], acth[:, parity, k, toks], actl[:, parity, k, toks], wh[:, k, cols],
                                      wl[:, k, cols], k == 0, k == 1)
                    if o < 7:
                        filled(ins, "ffn", ("d", o))
                used(ins)
            hidden("g", "ffn_in", "g0", 0)
            hidden("u", "ffn_in", "u0", 0)
            hidden("g", "ffn_in", "g1", 1)
            with pe.Fori(0, 4) as it:
                for w in range(2):
                    ku, kd, kg = LOOP_KEYS[w]
                    hidden("u", "ffn_loop", ku, it * 2 + (1 + w), it)
                    down("ffn_loop", kd, it * 2 + w, w, it)
                    hidden("g", "ffn_loop", kg, it * 2 + (2 + w), it)
            hidden("u", "ffn_out", "u9", 9)
            down("ffn_out", "d8", 8, 0)
            hidden("g", "ffn_out", "g10", 10)
            hidden("u", "ffn_out", "u10", 10)
            down("ffn_out", "d9", 9, 1)
            down("ffn_out", "d10", 10, 0)
            norm(2)
            for j in range(6):
                project("cd_in", [(j, min(256, CDIN - 256 * j))], 8, CD_TILES[j], tok(H1hi, H1lo), lambda t: (j, t),
                        None if j else h_ready[2])
            pe.wait_ge(cn_ready, 6)
            for b_ in range(3):
                b = bank(pe, "cq", b_)
                for a_ in range(2):
                    ins = T.transpose(b[:, a_ * P:(a_ + 1) * P], Zx[:, a_, CQ0 + b_ * P:CQ0 + (b_ + 1) * P], ident[:])
                filled(ins, "cq", b_)
            for b_ in range(2):
                b = bank(pe, "ckv", b_)
                for t in range(NT):
                    src = Zx[:, t - 2, CKV0 + b_ * P:CKV0 + (b_ + 1) * P] if t >= 2 else Zt[:, t, 384 + b_ * P:384 + (b_ + 1) * P]
                    ins = T.transpose(b[:, t * P:(t + 1) * P], src, ident[:])
                filled(ins, "ckv", b_)
            pe.wait_ge(cqn_ready, 5)
            for h in range(2):
                project("uq", [(h, 384)], 3, range(2), tok(H1hi, H1lo), lambda t: (h, t))
            wh, wl = slab(pe, "ukv", 0, (2, D))
            for t in range(NT):
                for h in range(2):
                    b = bank(pe, "ukv", (t, h))
                    for k in range(2):
                        toks, cols = slice(t * P, (t + 1) * P), slice(512 * h, 512 * h + 512)
                        ins = product(pe, b[:], H1hi[:, 4 + k, toks], H1lo[:, 4 + k, toks], wh[:, k, cols], wl[:, k, cols],
                                      k == 0, k == 1)
                    if (t, h) != (3, 1):
                        filled(ins, "ukv", (t, h))
            used(ins)
            pe.wait_ge(qk_ready, 4)
            b = bank(pe, "heads", "kc")
            for t in range(NT):
                ins = T.transpose(b[:, t * P:(t + 1) * P], Zx[:, t - 2, 512:640] if t >= 2 else Zt[:, t, 0:128], ident[:])
            filled(ins, "heads", "kc")
            for i in range(2):
                b = bank(pe, "heads", ("qc", i))
                for j in range(2):
                    for a_ in range(2):
                        c0 = (2 * j + a_) * P
                        ins = T.transpose(b[:, c0:c0 + P], Zx[:, a_, (2 * i + j) * P:(2 * i + j + 1) * P], ident[:])
                filled(ins, "heads", ("qc", i))
            pe.wait_ge(kr_ready, 2)
            b = bank(pe, "heads", "kr")
            for t in range(NT):
                ins = T.transpose(b[0:32, t * P:(t + 1) * P], Zx[:, t - 2, KR0:CDIN] if t >= 2 else Zt[:, t, 640:672], ident[:])
            filled(ins, "heads", "kr")
            for h in range(8):
                b = bank(pe, "heads", ("kd", h))
                for t in range(NT):
                    await_emptied(pe, "ukv", (t, h // 4))
                    ins = T.transpose(b[0:64, t * P:(t + 1) * P], kv[:, t, h * P:h * P + 64], ident[:])
                filled(ins, "heads", ("kd", h))
            pe.wait_ge(rope_ready, 2)
            for i in range(4):
                b = bank(pe, "heads", ("qd", i))
                for j in range(2):
                    for a_ in range(2):
                        c0, h = (2 * j + a_) * P, 2 * i + j
                        ins = T.transpose(b[0:96, c0:c0 + P], qd[:, a_, 96 * h:96 * h + 96], ident[:])
                filled(ins, "heads", ("qd", i))
            for key in ["kc", "kr"] + [("qc", i) for i in range(2)] + [("kd", h) for h in range(8)] + [("qd", i) for i in range(4)]:
                await_emptied(pe, "heads", key)

            for i in range(34):
                if i < 32:
                    br, h, a_ = unit(i)
                    toks = slice(a_ * P, (a_ + 1) * P)
                    rows = slice(64 * (h // 4), 64 * (h // 4) + 64)
                    q_, k_ = (qdT[0:96, h, toks], kdT[0:96, h, :]) if br else (qcT[rows, h % 4, toks], kcT[rows, :])
                    filled(T.matmul(bank(pe, "att", ("s", i))[:], q_, k_, start=True, stop=True), "att", ("s", i))
                if i % 4 == 0 and i >= 4:
                    columns_of(1, late_block(i - 4))
                if i < 32 and i % 2 == 0:
                    rows_of(1, late_block(i - i % 4), i % 4 // 2)
                if 2 <= i:
                    br, h, a_ = unit(i - 2)
                    await_emptied(pe, "att", ("t", i - 2))
                    b = bank(pe, "att", ("o", i - 2))
                    for t in range(NT):
                        if br:
                            val = kv[:, t, h * P + 64:(h + 1) * P]
                        else:
                            c0 = (h // 4) * 64
                            val = Zx[:, t - 2, 640 + c0:704 + c0] if t >= 2 else Zt[:, t, 128 + c0:192 + c0]
                        ins = T.matmul(b[:, 0:64], pT[:, i % 2, t * P:(t + 1) * P], val, start=(t == 0), stop=(t == 3))
                    filled(ins, "att", ("o", i - 2))
                if 1 <= i < 33:
                    await_emptied(pe, "att", ("s", i - 1))
                    b = bank(pe, "att", ("t", i - 1))
                    for t in range(NT):
                        ins = T.transpose(b[:, t * P:(t + 1) * P], pexp[:, (i - 1) % 2, t * P:(t + 1) * P], ident[:])
                    filled(ins, "att", ("t", i - 1))
            for i in (30, 31):
                await_emptied(pe, "att", ("o", i))
            for b_ in range(4):
                b = bank(pe, "oT", b_)
                for j in range(2):
                    for a_ in range(2):
                        c0 = (2 * j + a_) * P
                        ins = T.transpose(b[:, c0:c0 + P], X[:, a_, (2 * b_ + j) * P:(2 * b_ + j + 1) * P], ident[:])
                filled(ins, "oT", b_)
            for b_ in range(4):
                await_emptied(pe, "oT", b_)
            for h in range(2):
                project("cd_out", [((h, 0), 512), ((h, 1), 512)], 4, range(2), tok(oTh, oTl), lambda t: (h, t))
            norm(3)
            for k in range(8):
                await_emptied(pe, "norm3", k)
            pe.wait_ge(experts_in, 16 * 5)
            b = bank(pe, "route", "logits")
            for t in range(2):
                for k in range(KD):
                    ins = T.matmul(b[:, t * NE:(t + 1) * NE], h2T[:, k, t * P:(t + 1) * P], router[:, k, :],
                                   start=(k == 0), stop=(k == KD - 1))
            filled(ins, "route", "logits")
            for b_ in range(4):
                b = bank(pe, "route", ("back", b_))
                for kk in range(4):
                    ins = T.transpose(b[:, kk * P:(kk + 1) * P],
                                      h2T[:, (b_ % 2) * 4 + kk, (b_ // 2) * P:(b_ // 2 + 1) * P], ident[:])
                filled(ins, "route", ("back", b_))
            pe.wait_ge(chosen_ready, 2)
            b = bank(pe, "route", "cum")
            T.matmul(b[:, 0:8], tri[:], chosen[:, 0, :], start=True, stop=True)
            T.matmul(b[:, 8:16], ones[:], chosen[:, 0, :], start=True, stop=False)
            T.matmul(b[:, 8:16], tri[:], chosen[:, 1, :], start=False, stop=True)
            T.matmul(b[:, 16:24], ones[:], chosen[:, 0, :], start=True, stop=False)
            filled(T.matmul(b[:, 16:24], ones[:], chosen[:, 1, :], start=False, stop=True), "route", "cum")
            for b_ in range(4):
                await_emptied(pe, "route", ("back", b_))

            def gather(r, stage, w, par, placed, it=0):
                pe.wait_ge(p_ready[r], placed)
                for part, src in (("xh", h2h), ("xl", h2l)):
                    for h in range(2):
                        b = bank(pe, stage, (part, w, h), it)
                        for kk in range(4):
                            k = 4 * h + kk
                            for t in range(2):
                                ins = T.matmul(b[:, kk * P:(kk + 1) * P], src[:, t, k * P:(k + 1) * P], Pm[:, par, t, :],
                                               start=(t == 0), stop=(t == 1))
                        filled(ins, stage, (part, w, h))
                b = bank(pe, stage, ("pt", w), it)
                for t in range(2):
                    ins = T.transpose(b[:, t * P:(t + 1) * P], Pm[:, par, t, :].bitcast(F32), ident[:])
                filled(ins, stage, ("pt", w))

            def features(st, kind, w, c, it):
                n_ = 512 if c < 5 else 256
                b = bank(pe, st, (kind, w, c), it)
                first = (4 * c + (2 if kind == "u" else 0)) if c < 5 else (20 if kind == "g" else 21)
                parts = 2 if c < 5 else 1
                for q in range(parts):
                    blocks = KD // parts
                    wh, wl = slab(pe, st, (w, first + q), (blocks, n_), it)
                    for k in range(blocks):
                        kk = q * blocks + k
                        ins = product(pe, b[:, 0:n_], xgh[:, kk, :], xgl[:, kk, :], wh[:, k, :], wl[:, k, :],
                                      kk == 0, kk == KD - 1)
                    used(ins)

            def turn(st, w, c, it):
                await_emptied(pe, st, ("u", w, c), it)
                b = bank(pe, st, ("t", w, c), it)
                for j in range(4 if c < 5 else 2):
                    ins = T.transpose(b[:, j * P:(j + 1) * P], ame[:, c % 2, j * P:(j + 1) * P], ident[:])
                filled(ins, st, ("t", w, c))

            def down_e(st, w, it):
                out_banks = [bank(pe, st, ("d", w, h), it) for h in range(2)]
                for j in range(11):
                    await_emptied(pe, st, ("t", w, (2 * j + 1) // 4), it)
                    wh, wl = slab(pe, st, (w, 22 + j), (2, D), it)
                    for h in range(2):
                        for k in range(2):
                            kk, cols = 2 * j + k, slice(512 * h, 512 * h + 512)
                            ins = product(pe, out_banks[h][:], aTh[:, kk, :], aTl[:, kk, :], wh[:, k, cols], wl[:, k, cols],
                                          kk == 0, kk == 21)
                        if j == 10 and h == 0:
                            filled(ins, st, ("d", w, 0))
                    used(ins)

            def scatter(st, w, it):
                for h in range(2):
                    await_emptied(pe, st, ("d", w, h), it)
                for o in range(4):
                    t, h = o // 2, o % 2
                    b = bank(pe, st, ("y", w, o), it)
                    T.matmul(b[:], PT[:, w, t, :], yeh[:, h, :], start=True, stop=False)
                    filled(T.matmul(b[:], PT[:, w, t, :], yel[:, h, :], start=False, stop=True), st, ("y", w, o))

            def expert(st, w, it):
                for key in (("xl", 1 - w, 1), ("pt", 1 - w)):
                    if st == "over" or w == 1:
                        await_emptied(pe, st, key, it)
                for c in range(6):
                    features(st, "g", w, c, it)
                    features(st, "u", w, c, it)
                    if w == 1 and c == 0:
                        scatter(st, 0, it)
                    if c:
                        turn(st, w, c - 1, it)
                if st == "moe":
                    gather(0, st, w, 1 - w, it * 4 + (2 * w + 4), it)
                turn(st, w, 5, it)
                down_e(st, w, it)
            gather(0, "first", 1, 0, 2)
            for key in (("xl", 1, 1), ("pt", 1)):
                await_emptied(pe, "first", key)
            with pe.Fori(0, NE // 2) as it:
                expert("moe", 0, it)
                expert("moe", 1, it)
                scatter("moe", 1, it)
                for key in (("xl", 1, 1), ("pt", 1)):
                    await_emptied(pe, "moe", key, it)
            pe.wait_ge(routed, 1)
            with pe.Fori(0, OVER) as j:
                more = pe.value_load(over_i[0:1, 0, bass.ds(j, 1)], min_val=0, max_val=NE)
                with pe.If(more > 0):
                    gather(1, "over", 1, 0, j * 2 + 2, j)
                    expert("over", 0, j)
                    scatter("over", 0, j)


_INS = ["x", "c", "ctx", "c_ctx", "ada_w", "ada_b", "ab_w_in", "a_v_gain", "a_w_s", "a_b_s", "b_w_pool", "b_scale",
        "ab_w_out", "ffn_w_gate", "ffn_w_up", "ffn_w_down", "cd_w_in", "c_q_gain", "c_k_gain", "d_cq_gain",
        "d_ckv_gain", "d_w_uq", "d_w_ukv", "cd_w_out", "moe_router", "moe_w_gate", "moe_w_up", "moe_w_down", "final_gain"]


def kernel(**inputs):
    import concourse.bacc as bacc
    from concourse.bass_utils import run_bass_kernel_spmd

    nc = bacc.Bacc("TRN2", target_bir_lowering=False, num_devices=1)
    arrays, args = {}, {}
    given = {name: np.ascontiguousarray(inputs[name]) for name in _INS}
    given.update(shape_tables())
    for name, value in given.items():
        arrays[f"in_{name}_dram"] = value
        args[name] = nc.dram_tensor(f"in_{name}_dram", value.shape, mybir.dt.from_np(value.dtype), kind="ExternalInput").ap()
    out = nc.dram_tensor("out_0_dram", (1, SEQ, D), F32, kind="ExternalOutput").ap()
    build(nc, args, out)
    r = run_bass_kernel_spmd(nc, [arrays], core_ids=[0])
    return r.results[0]["out_0_dram"]
```
